# Optimizing a Trainium2 kernel written in Bass

```python
import math
import jax, jax.numpy as jnp
from jax import lax
import numpy as np
import jax
import jax.numpy as jnp

D_MODEL = 1024
BATCH = 1
SEQ = 256
DEPTH = 1

N_META = 16
CONV_WIDTH = 3
D_CONV = D_MODEL
CONV_GROUPS = 16
SB_HEAD_DIM = 64
SB_HEADS = 16
D_ATTN = SB_HEADS * SB_HEAD_DIM
N_BRANCH = 2
D_IN = 3 * D_CONV + 3 * D_ATTN + N_BRANCH * D_MODEL
D_FF = 2816
Q_BLOCK = 128
RMS_EPS = 1e-6


def rms_norm(x, g):
    xf = x.astype(jnp.float32)
    y = xf * lax.rsqrt(jnp.mean(xf * xf, axis=-1, keepdims=True) + RMS_EPS)
    return (y * g.astype(jnp.float32)).astype(x.dtype)

def causal_dwconv(x, w):
    k, c = w.shape
    return lax.conv_general_dilated(
        x, w.reshape(k, 1, c).astype(x.dtype),
        window_strides=(1,), padding=[(k - 1, 0)],
        dimension_numbers=("NWC", "WIO", "NWC"),
        feature_group_count=c)

def stick_breaking_attention(q, k, v):
    seq_len = q.shape[1]
    scale = 1.0 / math.sqrt(q.shape[-1])
    bounds = [(0, N_META)] + [(s, min(s + Q_BLOCK, seq_len))
                              for s in range(N_META, seq_len, Q_BLOCK)]
    outs = []
    for q0, q1 in bounds:
        qb = q[:, q0:q1]
        kb = k[:, :q1]
        vb = v[:, :q1].astype(jnp.float32)
        z = jnp.einsum("bqhd,bkhd->bhqk", qb, kb,
                       preferred_element_type=jnp.float32) * scale
        t_idx = jnp.arange(q0, q1)[:, None]
        s_idx = jnp.arange(q1)[None, :]
        causal = s_idx < t_idx
        log_beta = jax.nn.log_sigmoid(z)
        log_fail = jnp.where(causal, log_beta - z, 0.0)
        survive = lax.cumsum(log_fail, axis=3, reverse=True) - log_fail
        a = jnp.where(causal, jnp.exp(log_beta + survive), 0.0)
        o = jnp.einsum("bhqk,bkhd->bqhd", a, vb)
        outs.append(o.astype(v.dtype))
    return jnp.concatenate(outs, axis=1)

def hybrid_mixer(xn, w_in, conv_w_mix, w_proj_conv, w_proj_attn, b_gate, w_out):
    bsz, seq_len, _ = xn.shape
    h = xn @ w_in
    splits = np.cumsum([D_CONV, D_CONV, D_CONV, D_ATTN, D_ATTN, D_ATTN, D_MODEL])
    b_c, c_c, h_c, q, k, v, g_conv, g_attn = jnp.split(h, list(splits), axis=-1)

    y_conv = b_c * causal_dwconv(c_c * h_c, conv_w_mix)
    branch_conv = y_conv @ w_proj_conv

    hd = (bsz, seq_len, SB_HEADS, SB_HEAD_DIM)
    o = stick_breaking_attention(q.reshape(hd), k.reshape(hd), v.reshape(hd))
    branch_attn = o.reshape(bsz, seq_len, D_ATTN) @ w_proj_attn

    gate_conv = jax.nn.sigmoid(g_conv + b_gate[0])
    gate_attn = jax.nn.sigmoid(g_attn + b_gate[1])
    merged = gate_conv * branch_conv + gate_attn * branch_attn
    return merged @ w_out

def conv_gated_mlp(xn, w_up_gate, conv_w_ffn, w_down):
    u, g = jnp.split(xn @ w_up_gate, 2, axis=-1)
    u = causal_dwconv(u, conv_w_ffn)
    return (jax.nn.gelu(u) * g) @ w_down

def first_inputs(seed: int = 0) -> dict:
    key = jax.random.key(seed)
    ks = jax.random.split(key, 16)
    f32 = jnp.float32

    def normal(k, shape, scale):
        return jax.random.normal(k, shape, f32) * scale

    def gain(k):
        return 1.0 + normal(k, (DEPTH, D_MODEL), 0.05)

    return {
        "x": normal(ks[0], (BATCH, SEQ, D_MODEL), 1.0),
        "meta_tokens": normal(ks[1], (N_META, D_MODEL), 1.0),
        "g_pre_mix": gain(ks[2]),
        "w_in": normal(ks[3], (DEPTH, D_MODEL, D_IN), D_MODEL ** -0.5),
        "conv_w_mix": normal(ks[4], (DEPTH, CONV_WIDTH, D_CONV), CONV_WIDTH ** -0.5),
        "w_proj_conv": normal(ks[5], (DEPTH, D_CONV, D_MODEL), D_CONV ** -0.5),
        "w_proj_attn": normal(ks[6], (DEPTH, D_ATTN, D_MODEL), D_ATTN ** -0.5),
        "b_gate": normal(ks[7], (DEPTH, N_BRANCH, D_MODEL), 0.02),
        "w_out": normal(ks[8], (DEPTH, D_MODEL, D_MODEL), D_MODEL ** -0.5),
        "g_post_mix": gain(ks[9]),
        "g_pre_ffn": gain(ks[10]),
        "w_up_gate": normal(ks[11], (DEPTH, D_MODEL, 2 * D_FF), D_MODEL ** -0.5),
        "conv_w_ffn": normal(ks[12], (DEPTH, CONV_WIDTH, D_FF), CONV_WIDTH ** -0.5),
        "w_down": normal(ks[13], (DEPTH, D_FF, D_MODEL), D_FF ** -0.5),
        "g_post_ffn": gain(ks[14]),
    }

def first_block(x, meta_tokens, g_pre_mix, w_in, conv_w_mix, w_proj_conv, w_proj_attn,
              b_gate, w_out, g_post_mix, g_pre_ffn, w_up_gate, conv_w_ffn, w_down,
              g_post_ffn):
    bsz = x.shape[0]
    meta = jnp.broadcast_to(meta_tokens[None].astype(x.dtype), (bsz, N_META, D_MODEL))
    h = jnp.concatenate([meta, x], axis=1)
    for layer in range(DEPTH):
        mix = hybrid_mixer(rms_norm(h, g_pre_mix[layer]), w_in[layer], conv_w_mix[layer],
                           w_proj_conv[layer], w_proj_attn[layer], b_gate[layer],
                           w_out[layer])
        h = h + rms_norm(mix, g_post_mix[layer])
        ffn = conv_gated_mlp(rms_norm(h, g_pre_ffn[layer]), w_up_gate[layer],
                             conv_w_ffn[layer], w_down[layer])
        h = h + rms_norm(ffn, g_post_ffn[layer])
    return h[:, N_META:, :]


DEPTH_2 = 2

SSD_WIDTH = D_MODEL
SSD_HEAD_DIM = 64
SSD_HEADS = SSD_WIDTH // SSD_HEAD_DIM
SSD_GROUPS = 2
SSD_HEADS_PER_GROUP = SSD_HEADS // SSD_GROUPS
SSD_STATE = 64
SSD_CONV = 4
SSD_CHUNK = 128
SSD_CONV_DIM = SSD_WIDTH + 2 * SSD_GROUPS * SSD_STATE
GLA_HEADS = 8
GLA_VALUE_WIDTH = D_MODEL
GLA_KEY_WIDTH = D_MODEL // 2
GLA_HEAD_K = GLA_KEY_WIDTH // GLA_HEADS
GLA_HEAD_V = GLA_VALUE_WIDTH // GLA_HEADS
GLA_GATE_RANK = 16
GLA_GATE_NORMALIZER = 16.0
GLA_CHUNK = 64
EVEN_SPLITS = (SSD_WIDTH, SSD_CONV_DIM, SSD_HEADS, GLA_KEY_WIDTH, GLA_KEY_WIDTH, GLA_VALUE_WIDTH, GLA_GATE_RANK, GLA_VALUE_WIDTH)
EVEN_IN_WIDTH = sum(EVEN_SPLITS)
EVEN_MIX_WIDTH = SSD_WIDTH + GLA_VALUE_WIDTH
MOBA_HEADS = 16
MOBA_HEAD_DIM = 64
MOBA_WIDTH = MOBA_HEADS * MOBA_HEAD_DIM
MOBA_BLOCK = 256
MOBA_TOPK = 3
MOBA_Q_CHUNK = 32
ODD_IN_WIDTH = 4 * MOBA_WIDTH
N_EVEN = (DEPTH_2 + 1) // 2
N_ODD = DEPTH_2 // 2


def rms_norm_2(x, w):
    x32 = x.astype(jnp.float32)
    y = x32 * lax.rsqrt(jnp.mean(x32 * x32, axis=-1, keepdims=True) + RMS_EPS)
    return y * w.astype(jnp.float32)

def split_cols(u, sizes):
    cuts = [int(c) for c in np.cumsum(sizes)[:-1]]
    return jnp.split(u, cuts, axis=-1)

def causal_depthwise_conv(u, w, b):
    k_width = w.shape[0]
    y = lax.conv_general_dilated(u, w.astype(u.dtype)[:, None, :], window_strides=(1,), padding=[(k_width - 1, 0)], dimension_numbers=('NWC', 'WIO', 'NWC'), feature_group_count=u.shape[-1])
    return y + b.astype(u.dtype)

def ssd_chunked_scan(xs, dt, a, bm, cm, d_skip):
    b, L, G, E, P = xs.shape
    N = bm.shape[-1]
    Q = SSD_CHUNK
    nc = L // Q
    x_c = xs.reshape(b, nc, Q, G, E, P)
    dt_c = dt.reshape(b, nc, Q, G, E)
    xdt = x_c * dt_c[..., None]
    b_c = bm.reshape(b, nc, Q, G, N)
    c_c = cm.reshape(b, nc, Q, G, N)
    a_cs = jnp.cumsum(dt_c * a, axis=2)
    a_t = jnp.moveaxis(a_cs, 2, -1)
    seg = a_t[..., :, None] - a_t[..., None, :]
    causal = jnp.tril(jnp.ones((Q, Q), dtype=bool))
    decay_ij = jnp.exp(jnp.where(causal, seg, -jnp.inf))
    cb = jnp.einsum('bcign,bcjgn->bcgij', c_c, b_c)
    y_diag = jnp.einsum('bcgeij,bcjgep->bcigep', cb[:, :, :, None] * decay_ij, xdt)
    a_last = a_cs[:, :, -1]
    decay_to_end = jnp.exp(a_last[:, :, None] - a_cs)
    chunk_states = jnp.einsum('bcjgn,bcjge,bcjgep->bcgepn', b_c, decay_to_end, xdt)

    def carry_state(h, inp):
        chunk_decay, s = inp
        return chunk_decay[..., None, None] * h + s, h

    _, prev_states = lax.scan(carry_state, jnp.zeros_like(chunk_states[:, 0]), (jnp.moveaxis(jnp.exp(a_last), 1, 0), jnp.moveaxis(chunk_states, 1, 0)))
    prev_states = jnp.moveaxis(prev_states, 0, 1)
    y_off = jnp.einsum('bcign,bcgepn->bcigep', c_c, prev_states) * jnp.exp(a_cs)[..., None]
    y = y_diag + y_off + d_skip[:, :, None] * x_c
    return y.reshape(b, L, G * E * P)

def gla_chunked(q, k, v, log_decay):
    b, L, H, dk = q.shape
    dv = v.shape[-1]
    C = GLA_CHUNK
    n = L // C
    q = q.reshape(b, n, C, H, dk)
    k = k.reshape(b, n, C, H, dk)
    v = v.reshape(b, n, C, H, dv)
    gcs = jnp.cumsum(log_decay.reshape(b, n, C, H, dk), axis=2)
    ref = gcs[:, :, C // 2:C // 2 + 1]
    scores = jnp.einsum('bnihd,bnjhd->bnhij', q * jnp.exp(gcs - ref), k * jnp.exp(ref - gcs))
    causal = jnp.tril(jnp.ones((C, C), dtype=bool))
    scores = jnp.where(causal, scores, 0.0)
    o_intra = jnp.einsum('bnhij,bnjhv->bnihv', scores, v)
    g_last = gcs[:, :, -1]
    chunk_kv = jnp.einsum('bnjhd,bnjhv->bnhdv', k * jnp.exp(g_last[:, :, None] - gcs), v)

    def carry_state(s, inp):
        decay, kv = inp
        return decay[..., None] * s + kv, s

    _, prev_states = lax.scan(carry_state, jnp.zeros_like(chunk_kv[:, 0]), (jnp.moveaxis(jnp.exp(g_last), 1, 0), jnp.moveaxis(chunk_kv, 1, 0)))
    prev_states = jnp.moveaxis(prev_states, 0, 1)
    o_inter = jnp.einsum('bnihd,bnhdv->bnihv', q * jnp.exp(gcs), prev_states)
    return (o_intra + o_inter).reshape(b, L, H, dv)

def ssd_gla_layer(x, norm_w, w_in, conv_w, conv_b, a_log, dt_bias, d_skip, ssd_norm_w, gate_w2, gate_b, gla_norm_w, w_out):
    bsz, L, _ = x.shape
    h = rms_norm_2(x, norm_w)
    u = h @ w_in.astype(jnp.float32)
    z_a, xbc, dt_raw, q_b, k_b, v_b, gate_lr, g_b = split_cols(u, EVEN_SPLITS)
    xbc = jax.nn.silu(causal_depthwise_conv(xbc, conv_w, conv_b))
    xs, bm, cm = split_cols(xbc, (SSD_WIDTH, SSD_GROUPS * SSD_STATE, SSD_GROUPS * SSD_STATE))
    xs = xs.reshape(bsz, L, SSD_GROUPS, SSD_HEADS_PER_GROUP, SSD_HEAD_DIM)
    bm = bm.reshape(bsz, L, SSD_GROUPS, SSD_STATE)
    cm = cm.reshape(bsz, L, SSD_GROUPS, SSD_STATE)
    dt = jax.nn.softplus(dt_raw + dt_bias.astype(jnp.float32)).reshape(bsz, L, SSD_GROUPS, SSD_HEADS_PER_GROUP)
    a = -jnp.exp(a_log.astype(jnp.float32)).reshape(SSD_GROUPS, SSD_HEADS_PER_GROUP)
    d = d_skip.astype(jnp.float32).reshape(SSD_GROUPS, SSD_HEADS_PER_GROUP)
    y_a = ssd_chunked_scan(xs, dt, a, bm, cm, d)
    y_a = rms_norm_2(y_a * jax.nn.silu(z_a), ssd_norm_w)
    q_b = q_b.reshape(bsz, L, GLA_HEADS, GLA_HEAD_K) * (GLA_HEAD_K ** -0.5)
    k_b = k_b.reshape(bsz, L, GLA_HEADS, GLA_HEAD_K)
    v_b = v_b.reshape(bsz, L, GLA_HEADS, GLA_HEAD_V)
    log_decay = jax.nn.log_sigmoid(gate_lr @ gate_w2.astype(jnp.float32) + gate_b.astype(jnp.float32)) / GLA_GATE_NORMALIZER
    log_decay = log_decay.reshape(bsz, L, GLA_HEADS, GLA_HEAD_K)
    o_b = gla_chunked(q_b, k_b, v_b, log_decay)
    o_b = rms_norm_2(o_b, gla_norm_w).reshape(bsz, L, GLA_VALUE_WIDTH) * jax.nn.silu(g_b)
    out = jnp.concatenate([y_a, o_b], axis=-1) @ w_out.astype(jnp.float32)
    return x + out.astype(x.dtype)

def moba_attention(q, k, v):
    b, H, L, d = q.shape
    nb = -(-L // MOBA_BLOCK)
    lp = nb * MOBA_BLOCK
    pad = ((0, 0), (0, 0), (0, lp - L), (0, 0))
    q = jnp.pad(q * (d ** -0.5), pad)
    k = jnp.pad(k, pad)
    v = jnp.pad(v, pad)
    kb = k.reshape(b, H, nb, MOBA_BLOCK, d)
    vb = v.reshape(b, H, nb, MOBA_BLOCK, d)
    k_mean = jnp.mean(kb, axis=3)
    gate = jnp.einsum('bhqd,bhnd->bhqn', q, k_mean).astype(jnp.float32)
    n_past_all = jnp.arange(lp) // MOBA_BLOCK
    fully_past = jnp.arange(nb)[None, :] < n_past_all[:, None]
    gate = jnp.where(fully_past, gate, -jnp.inf)
    k_sel = min(MOBA_TOPK, nb)
    _, top_idx = lax.top_k(gate, k_sel)
    bi = jnp.arange(b)[:, None, None]
    hi = jnp.arange(H)[None, :, None]

    def attend_chunk(start):
        qc = lax.dynamic_slice_in_dim(q, start, MOBA_Q_CHUNK, axis=2)
        idx_c = lax.dynamic_slice_in_dim(top_idx, start, MOBA_Q_CHUNK, axis=2)
        pos = start + jnp.arange(MOBA_Q_CHUNK)
        n_past = pos // MOBA_BLOCK
        logits = []
        for s in range(k_sel):
            ks = kb[bi, hi, idx_c[..., s]]
            ls = jnp.einsum('bhqd,bhqkd->bhqk', qc, ks).astype(jnp.float32)
            logits.append(jnp.where((s < n_past)[:, None], ls, -jnp.inf))
        own = start // MOBA_BLOCK
        ko = lax.dynamic_index_in_dim(kb, own, axis=2, keepdims=False)
        vo = lax.dynamic_index_in_dim(vb, own, axis=2, keepdims=False)
        lo = jnp.einsum('bhqd,bhkd->bhqk', qc, ko).astype(jnp.float32)
        key_pos = own * MOBA_BLOCK + jnp.arange(MOBA_BLOCK)
        logits.append(jnp.where(key_pos[None, :] <= pos[:, None], lo, -jnp.inf))
        p = jax.nn.softmax(jnp.concatenate(logits, axis=-1), axis=-1)
        p_parts = jnp.split(p, k_sel + 1, axis=-1)
        out = jnp.einsum('bhqk,bhkd->bhqd', p_parts[-1].astype(vo.dtype), vo)
        for s in range(k_sel):
            vs = vb[bi, hi, idx_c[..., s]]
            out = out + jnp.einsum('bhqk,bhqkd->bhqd', p_parts[s].astype(vs.dtype), vs)
        return out

    starts = jnp.arange(lp // MOBA_Q_CHUNK) * MOBA_Q_CHUNK
    outs = lax.map(attend_chunk, starts)
    out = jnp.moveaxis(outs, 0, 2).reshape(b, H, lp, d)
    return out[:, :, :L]

def moba_layer(x, norm_w, w_in, w_out):
    bsz, L, _ = x.shape
    h = rms_norm_2(x, norm_w)
    u = h @ w_in.astype(jnp.float32)
    q, k, v, z = split_cols(u, (MOBA_WIDTH, MOBA_WIDTH, MOBA_WIDTH, MOBA_WIDTH))
    to_heads = lambda t: t.reshape(bsz, L, MOBA_HEADS, MOBA_HEAD_DIM).transpose(0, 2, 1, 3)
    o = moba_attention(to_heads(q), to_heads(k), to_heads(v))
    o = o.transpose(0, 2, 1, 3).reshape(bsz, L, MOBA_WIDTH) * jax.nn.silu(z)
    return x + (o @ w_out.astype(jnp.float32)).astype(x.dtype)

def second_inputs(seed: int = 0) -> dict:
    key = jax.random.key(seed)
    ks = jax.random.split(key, 20)
    nrm = jax.random.normal
    f32 = jnp.float32
    dt_init = jnp.exp(jax.random.uniform(ks[6], (N_EVEN, SSD_HEADS), f32, np.log(1e-3), np.log(1e-1)))
    return {
        'x': nrm(ks[0], (BATCH, SEQ, D_MODEL), f32),
        'even_norm': 1.0 + 0.02 * nrm(ks[1], (N_EVEN, D_MODEL), f32),
        'even_w_in': nrm(ks[2], (N_EVEN, D_MODEL, EVEN_IN_WIDTH), f32) * D_MODEL ** -0.5,
        'even_conv_w': nrm(ks[3], (N_EVEN, SSD_CONV, SSD_CONV_DIM), f32) * SSD_CONV ** -0.5,
        'even_conv_b': 0.02 * nrm(ks[4], (N_EVEN, SSD_CONV_DIM), f32),
        'even_a_log': jnp.log(jax.random.uniform(ks[5], (N_EVEN, SSD_HEADS), f32, 1.0, 16.0)),
        'even_dt_bias': dt_init + jnp.log(-jnp.expm1(-dt_init)),
        'even_d_skip': 1.0 + 0.1 * nrm(ks[7], (N_EVEN, SSD_HEADS), f32),
        'even_ssd_norm': 1.0 + 0.02 * nrm(ks[8], (N_EVEN, SSD_WIDTH), f32),
        'even_gate_w2': nrm(ks[9], (N_EVEN, GLA_GATE_RANK, GLA_KEY_WIDTH), f32) * GLA_GATE_RANK ** -0.5,
        'even_gate_b': 0.1 * nrm(ks[10], (N_EVEN, GLA_KEY_WIDTH), f32),
        'even_gla_norm': 1.0 + 0.02 * nrm(ks[11], (N_EVEN, GLA_HEAD_V), f32),
        'even_w_out': nrm(ks[12], (N_EVEN, EVEN_MIX_WIDTH, D_MODEL), f32) * EVEN_MIX_WIDTH ** -0.5,
        'odd_norm': 1.0 + 0.02 * nrm(ks[13], (N_ODD, D_MODEL), f32),
        'odd_w_in': nrm(ks[14], (N_ODD, D_MODEL, ODD_IN_WIDTH), f32) * D_MODEL ** -0.5,
        'odd_w_out': nrm(ks[15], (N_ODD, MOBA_WIDTH, D_MODEL), f32) * MOBA_WIDTH ** -0.5,
        'final_norm': 1.0 + 0.02 * nrm(ks[16], (D_MODEL,), f32),
    }

def second_block(x, even_norm, even_w_in, even_conv_w, even_conv_b, even_a_log, even_dt_bias, even_d_skip, even_ssd_norm, even_gate_w2, even_gate_b, even_gla_norm, even_w_out, odd_norm, odd_w_in, odd_w_out, final_norm):
    for layer in range(DEPTH_2):
        i = layer // 2
        if layer % 2 == 0:
            x = ssd_gla_layer(x, even_norm[i], even_w_in[i], even_conv_w[i], even_conv_b[i], even_a_log[i], even_dt_bias[i], even_d_skip[i], even_ssd_norm[i], even_gate_w2[i], even_gate_b[i], even_gla_norm[i], even_w_out[i])
        else:
            x = moba_layer(x, odd_norm[i], odd_w_in[i], odd_w_out[i])
    return rms_norm_2(x, final_norm).astype(x.dtype)


def setup_inputs(seed=0):
    out = dict(first_inputs(seed))
    for name, value in second_inputs(seed + 1).items():
        if name != "x":
            out[name + "_2"] = value
    return out


def reference(
    x, meta_tokens, g_pre_mix, w_in, conv_w_mix, w_proj_conv, w_proj_attn, b_gate, w_out,
    g_post_mix, g_pre_ffn, w_up_gate, conv_w_ffn, w_down, g_post_ffn, even_norm_2, even_w_in_2,
    even_conv_w_2, even_conv_b_2, even_a_log_2, even_dt_bias_2, even_d_skip_2, even_ssd_norm_2,
    even_gate_w2_2, even_gate_b_2, even_gla_norm_2, even_w_out_2, odd_norm_2, odd_w_in_2,
    odd_w_out_2, final_norm_2,
):
    x = first_block(
        x, meta_tokens, g_pre_mix, w_in, conv_w_mix, w_proj_conv, w_proj_attn, b_gate, w_out,
        g_post_mix, g_pre_ffn, w_up_gate, conv_w_ffn, w_down, g_post_ffn,
    )
    return second_block(
        x, even_norm_2, even_w_in_2, even_conv_w_2, even_conv_b_2, even_a_log_2, even_dt_bias_2,
        even_d_skip_2, even_ssd_norm_2, even_gate_w2_2, even_gate_b_2, even_gla_norm_2,
        even_w_out_2, odd_norm_2, odd_w_in_2, odd_w_out_2, final_norm_2,
    )


_drawn_inputs = setup_inputs


def setup_inputs(seed=0):
    import zlib

    import numpy as np

    out = dict(_drawn_inputs(seed))
    spreads = {}
    factors = {'b_gate': 7.532,
     'even_norm_2': 3.858,
     'even_conv_b_2': 6.131,
     'even_ssd_norm_2': 7.505,
     'even_gate_b_2': 5.795,
     'even_gla_norm_2': 8.0,
     'odd_norm_2': 8.0,
     'final_norm_2': 20.306,
     'even_d_skip_2': 22.345}
    for name, (base, spread) in spreads.items():
        noise = np.random.default_rng([zlib.crc32(name.encode()), seed]).standard_normal(out[name].shape)
        drawn = base * np.exp(spread * noise) if base else spread * noise
        out[name] = jnp.asarray(drawn.astype(out[name].dtype))
    for name, factor in factors.items():
        out[name] = (out[name] * factor).astype(out[name].dtype)
    return out
```

```python
from contextlib import ExitStack

import numpy as np
import concourse.bass as bass
from concourse import mybir

F32 = mybir.dt.float32
F32R = mybir.dt.float32r
I32 = mybir.dt.int32
ALU = mybir.AluOpType
ACT = mybir.ActivationFunctionType
AX_X = mybir.AxisListType.X

P = 128
D = 1024
KT = D // P
META = 16
L = 256
T = META + L
TA = META - 2
TC = TA - 2
NA = T - TA
FF = 2816
FT = FF // P
HEADS = 16
EPS = 1e-6

E_Z, E_XS, E_B, E_C, E_DT, E_Q, E_K, E_V, E_LR, E_G = 0, 1024, 2048, 2176, 2304, 2320, 2832, 3344, 4368, 4384
LR_ROW = 32

SEG = ((0, 0, TA), (NA, 128, 128), (NA + T - 128, 256, 256))
ZC = NA + (T - 128) + (T - 256)
CC = 256 + 128


def tiles_of_stream():
    out = []

    def w(stage, i, name, col, k=KT, width=P):
        out.append((stage, i, [(name, kt, col, width) for kt in range(k)], 1))

    def x(stage, i, name, col, n):
        out.append((stage, i, [(name, kt, col + c * P, P) for kt in range(KT) for c in range(2)], n))

    for i in range(KT):
        w("k", i, "w_in", 4096 + i * P)
    for i in range(4):
        x("v", i, "w_in", 5120 + i * 256, 3)
    for i in range(KT):
        w("q", i, "w_in", 3072 + i * P)
        w("c", i, "w_in", 1024 + i * P)
        w("h", i, "w_in", 2048 + i * P)
        w("b", i, "w_in", i * P)
    for i in range(KT):
        w("gc", i, "w_in", 6144 + i * P)
        w("ga", i, "w_in", 7168 + i * P)
        w("pc", i, "w_proj_conv", i * P)
        w("pa", i, "w_proj_attn", i * P)
    for i in range(KT):
        w("wo", i, "w_out", i * P)
    for i in range(FT):
        w("fu", i, "w_up_gate", i * P)
        w("fg", i, "w_up_gate", FF + i * P)
    for i in range(KT):
        w("fd", i, "w_down", i * P, FT)
    w("eb", 0, "even_w_in_2", E_B)
    w("ec", 0, "even_w_in_2", E_C)
    for i in range(KT):
        w("ex", i, "even_w_in_2", E_XS + i * P)
    w("es", 0, "small", 0)
    for i in range(4):
        w("eq", i, "even_w_in_2", E_Q + i * P)
    for i in range(4):
        w("ek", i, "even_w_in_2", E_K + i * P)
    for i in range(4):
        x("ev", i, "even_w_in_2", E_V + i * 256, 2)
    for i in range(KT):
        w("ez", i, "even_w_in_2", E_Z + i * P)
        w("eg", i, "even_w_in_2", E_G + i * P)
    for i in range(KT):
        w("eo", i, "even_w_out_2", i * P, 16)
    for i in range(KT):
        w("mk", i, "odd_w_in_2", 1024 + i * P)
    for i in range(4):
        x("mv", i, "odd_w_in_2", 2048 + i * 256, 2)
    for i in range(KT):
        w("mq", i, "odd_w_in_2", i * P)
        w("mz", i, "odd_w_in_2", 3072 + i * P)
    for i in range(KT):
        w("mo", i, "odd_w_out_2", i * P)
    return out


BPC = 8
CW = BPC * P
STREAM = tiles_of_stream()
FIRST_BLOCK, FIRST_OUT = {}, {}
_b = _o = 0
for _s, _i, _blocks, _n in STREAM:
    FIRST_BLOCK[_s, _i], FIRST_OUT[_s, _i] = _b, _o
    _b += len(_blocks)
    _o += _n
NBLOCKS, NOUTS = _b, _o
NCHUNKS = NBLOCKS // BPC
assert NCHUNKS * BPC == NBLOCKS
BLOCKS_OF = {(s, i): len(b) for s, i, b, n in STREAM}
OUTS_OF = {(s, i): n for s, i, b, n in STREAM}

PARAMS = {}
NPARAM = 0
for _name, _n in (("g_pre_mix", 8), ("g_post_mix", 8), ("g_pre_ffn", 8), ("g_post_ffn", 8), ("even_norm", 8),
                  ("ssd_norm", 8), ("odd_norm", 8), ("final_norm", 8), ("conv_mix", 24), ("b_gate", 16),
                  ("conv_ffn", 3 * FT), ("even_conv", 40), ("even_conv_b", 10), ("d_skip", 8), ("gate_b", 4),
                  ("gla_norm", 1), ("dt_bias", 1), ("a_log", 1)):
    PARAMS[_name] = NPARAM
    NPARAM += _n

RAW = 5
RING = 4


def build(nc, xT, params, weights, masks, gate_w2, out, scratch):
    with ExitStack() as ctx:
        def sb(name, cols, dt=F32):
            return ctx.enter_context(nc.sbuf_tensor(name, [P, cols], dt))

        sems = {}

        def S(name):
            if name not in sems:
                sems[name] = ctx.enter_context(nc.semaphore(name))
            return sems[name]

        raw = sb("raw_weights", RAW * CW)
        whi = sb("weights_hi", RING * CW, F32R)
        wlo = sb("weights_lo", RING * CW, F32R)
        xhi_t = sb("x_hi", KT * T, F32R)
        xlo_t = sb("x_lo", KT * T, F32R)
        YW = 3 * KT * NA
        yhi_t = sb("y_hi", YW, F32R)
        ylo_t = sb("y_lo", YW, F32R)
        h_t = sb("hidden", KT * T)
        prm = sb("params", NPARAM)
        msk = sb("masks", MASK_COLS)
        gw2 = sb("gate_w2", 512)
        rinv = sb("rinv", T)
        rpost = sb("rinv_post", T)
        rcol = sb("rinv_by_token", 4)
        arena = sb("arena", ARENA)
        acol = sb("decay_rate", 2)
        scans = sb("dt_and_cumsum", 256)

        ps = ctx.enter_context(nc.psum_tensor("ps", [P, 8, 512], F32))

        def v3(ap, n):
            return ap.rearrange("p (a b) -> p a b", a=n)

        xhi, xlo, H = v3(xhi_t[:], KT), v3(xlo_t[:], KT), v3(h_t[:], KT)
        yhi = yhi_t[:].rearrange("p (s a b) -> p s a b", s=3, a=KT)
        ylo = ylo_t[:].rearrange("p (s a b) -> p s a b", s=3, a=KT)
        fhi, flo = v3(yhi_t[:, 0:FT * L], FT), v3(ylo_t[:, 0:FT * L], FT)
        ehi, elo = v3(yhi_t[:, 0:16 * L], 16), v3(ylo_t[:, 0:16 * L], 16)
        CONV, ATT, MERGED = 0, 1, 2

        def mask(name):
            o, n = MASKS[name]
            return msk[:, o:o + n]

        def pcol(name, i=0):
            c = PARAMS[name] + i
            return prm[:, c:c + 1]

        class Area:
            def __init__(self, at=0):
                self.at = at

            def __call__(self, *shape):
                n = int(np.prod(shape))
                ap = arena[:, self.at:self.at + n]
                self.at += n
                assert self.at <= ARENA, self.at
                if len(shape) == 2:
                    ap = ap.rearrange("p (a b) -> p a b", a=shape[0])
                if len(shape) == 3:
                    ap = ap.rearrange("p (a b c) -> p a b c", a=shape[0], b=shape[1])
                return ap

        A1 = Area()
        keysT = A1(KT, 3 * P)
        vals = A1(3, D)
        qpair = A1(2, 2, T)
        sp = A1(2, ZC)
        fz = A1(2, ZC)
        aw = A1(2, ZC)
        cbuf = A1(2, T)
        chbuf = A1(2, T)
        cv = A1(2, NA)
        bb = A1(2, NA)
        gate = A1(4, NA)
        mm1 = A1(2, NA)
        A2 = Area()
        mout = A2(KT, T)
        A3 = Area(ARENA - KT * T)
        sq = A3(KT, T)
        assert A1.at <= ARENA - KT * T
        A4 = Area(KT * T)
        fu = A4(2, NA)
        fcv = A4(2, L)
        fgl = A4(2, L)
        fy = A4(2, L)
        A5 = Area()
        xs = A5(KT, L)
        gs = A5(KT, L)
        vb = A5(2, D)
        e_q = A5(4, L)
        e_k = A5(4, L)
        gcs = A5(4, L)
        cvo = A5(2, L)
        tkc = A5(2, P)
        small2 = A5(L)
        A6 = Area(A5.at)
        xd = A6(2, D)
        cb = A6(2, CC)
        A7 = Area(A6.at)
        bT = A7(L)
        cT = A7(2, L)
        sm = A7(L)
        scr2 = A7(2, L + 4)
        small1 = A7(L)
        acs = A7(L)
        gtmp = A7(2, L)
        A8 = Area(A6.at)
        bc = A8(2, 2, L)
        dec = A8(2, CC)
        zs = A8(2, L)
        sqy = A8(2, L)
        A10 = Area(A5.at)
        ka = A10(2, L)
        kb = A10(2, L)
        eg = A10(2, L)
        em = A10(L)
        qe = A10(2, 2, L)
        qg = A10(2, 2, L)
        klt = A10(2, 2, P)
        st = A10(3, P)
        sc = A10(2, L)
        osq = A10(512)
        orv = A10(512)
        A9 = Area()
        mkT = A9(KT, L)
        mval = A9(2, D)
        mqp = A9(2, 2, L)
        mzs = A9(2, L)
        mz = A9(2, L)
        ssm = A9(2, CC)
        pr = A9(2, CC)
        prT = A9(2, CC)
        mst = A9(2, 8)
        mo = A9(2, L)

        SSB = 7

        def bank(n):
            return ps[:, n, :]

        block = ctx.enter_context(nc.Block())

        class Steps:
            def __init__(self, eng, own):
                self.eng, self.own, self.n, self.last = eng, own, {}, None

            def sig(self, ins, name, k=1):
                ins.then_inc(S(name), k)
                self.n[name] = self.n.get(name, 0) + k
                self.last = (name, self.n[name])
                return ins

            def step(self, ins):
                return self.sig(ins, self.own)

            def settle(self):
                if self.last:
                    self.eng.wait_ge(S(self.last[0]), self.last[1])

        def need(eng, name, n):
            if n > 0:
                eng.wait_ge(S(name), n)

        freed = {}
        parts = 0
        for s_, i_, b_, n_ in STREAM:
            f = FIRST_BLOCK[s_, i_]
            for j in range(len(b_)):
                if (f + j) % BPC == BPC - 1:
                    if j == len(b_) - 1:
                        freed[(f + j) // BPC] = ("out_ready", FIRST_OUT[s_, i_] + n_)
                    elif n_ > 1:
                        parts += 1
                        freed[(f + j) // BPC] = ("chunk_read", parts)
                    else:
                        parts += 1
                        freed[(f + j) // BPC] = ("chunk_read", parts)

        def chunk_of(tile):
            f = FIRST_BLOCK[tile]
            return [c for c in range(f // BPC, (f + BLOCKS_OF[tile]) // BPC + 1)
                    if f <= c * BPC + BPC - 1 < f + BLOCKS_OF[tile]]

        @block.sync
        def _(sp_):
            for c in range(NCHUNKS):
                if c >= RAW:
                    sp_.wait_ge(S("lo_ready"), c - RAW + 1)
                s = c % RAW
                sp_.dma_start(raw[:, s * CW:(s + 1) * CW], weights[c]).then_inc(S(f"raw{s}"), 16)

        @block.gpsimd
        def _(pool):
            g = Steps(pool, "pool_step")
            g.sig(nc.gpsimd.memset(keysT[:, :, T:3 * P], 0.0), "zeroed")
            g.sig(nc.gpsimd.memset(vals[:, 2, :], 0.0), "zeroed")
            g.sig(nc.gpsimd.memset(qpair, 0.0), "zeroed")
            for i in range(FT):
                pool.wait_ge(S("gelu_ready"), i + 1)
                g.settle()
                g.sig(nc.gpsimd.tensor_tensor(fgl[:, i % 2, :], fgl[:, i % 2, :], rinv[:, META:T], ALU.mult),
                      "gelu_scaled")
                pool.wait_ge(S("ffn_hi"), i + 1)
                g.settle()
                g.sig(nc.gpsimd.tensor_tensor(flo[:, i, :], fy[:, i % 2, :], fhi[:, i, :].bitcast(F32),
                                              ALU.subtract), "ffn_split")
            pool.wait_ge(S("rms_ready"), 5)
            g.sig(nc.gpsimd.memset(cT, 0.0), "zeroed")
            g.sig(nc.gpsimd.memset(scr2[:, :, 0:3], 0.0), "zeroed")
            g.sig(nc.gpsimd.memset(scans[:], 0.0), "zeroed")
            pool.wait_ge(S("yz_ready"), KT)
            pool.wait_ge(S("sums_ready"), 6)
            g.sig(nc.gpsimd.memset(qe, 0.0), "zeroed")
            g.sig(nc.gpsimd.memset(qg, 0.0), "zeroed")
            g.sig(nc.gpsimd.memset(sc, 0.0), "zeroed")
            pool.wait_ge(S("h_ready"), 3 * KT)
            g.sig(nc.gpsimd.memset(mqp, 0.0), "zeroed")

        @block.scalar
        def _(act):
            a = Steps(act, "act_step")
            A = nc.scalar.activation

            def exp_and_ln():
                nc.scalar.preload_act_table_set("natural_log_exp_and_others")

            exp_and_ln()
            act.dma_start(prm[:], params).then_inc(S("load_params"), 16)
            act.dma_start(h_t[:], xT).then_inc(S("load_x"), 16)
            act.dma_start(msk[:], masks).then_inc(S("load_masks"), 16)
            act.dma_start(gw2[:], gate_w2).then_inc(S("load_gate"), 16)
            nxt = [0]

            def split_hi():
                c = nxt[0]
                nxt[0] += 1
                if c >= NCHUNKS:
                    return
                act.wait_ge(S(f"raw{c % RAW}"), 16 * (c // RAW + 1))
                if c >= RING:
                    act.wait_ge(S(freed[c - RING][0]), freed[c - RING][1])
                    act.wait_ge(S("lo_ready"), c - RING + 1)
                s = c % RING
                a.sig(A(whi[:, s * CW:(s + 1) * CW], raw[:, (c % RAW) * CW:(c % RAW + 1) * CW], ACT.Copy), "hi_ready")

            def feed(tile):
                for _ in chunk_of(tile):
                    split_hi()

            def x_high(n, gain, t0, base):
                for kt in range(KT):
                    if base is not None:
                        act.wait_ge(S("h_ready"), base + kt + 1)
                    a.sig(A(xhi[:, kt, t0:T], H[:, kt, t0:T], ACT.Copy, scale=pcol(gain, kt)), "x_hi")
                    a.sig(A(sq[:, kt, t0:T], H[:, kt, t0:T], ACT.Square), "sq_ready")

            def inverse_rms(dst, width, total, nth, src=None, cols=None):
                act.wait_ge(S("sums_ready"), nth)
                src = bank(SSB)[:, 0:width] if src is None else src
                a.step(A(dst, src, ACT.Ln, scale=1.0 / total, bias=epsb))
                a.settle()
                a.sig(A(dst, dst, ACT.Exp, scale=-0.5), "rms_ready")

            epsb = mask("eps")
            one = mask("one")
            act.wait_ge(S("load_params"), 16)
            act.wait_ge(S("load_masks"), 16)
            act.wait_ge(S("load_x"), 16)
            for _ in range(2):
                split_hi()
            x_high(0, "g_pre_mix", 0, None)
            for _ in range(RING - 2):
                split_hi()
            inverse_rms(rinv[:, 0:T], T, D, 1)
            for i in range(KT):
                feed(("k", i))
            for i in range(4):
                feed(("v", i))

            def softplus_part(h):
                act.wait_ge(S("z_ready"), h + 1)
                need(act, "f_ready", h - 1)
                a.settle()
                a.step(A(sp[:, h % 2, :], bank(4 + h % 2)[:, 0:ZC], ACT.Abs))
                a.settle()
                a.step(A(sp[:, h % 2, :], sp[:, h % 2, :], ACT.Exp, scale=-1.0))
                a.settle()
                a.sig(A(sp[:, h % 2, :], sp[:, h % 2, :], ACT.Ln, bias=one), "sp_ready")

            def weights_of(h):
                act.wait_ge(S("loga_taken"), h + 1)
                need(act, "av_ready", h - 1)
                a.sig(A(aw[:, h % 2, :], fz[:, h % 2, :], ACT.Exp), "a_ready")

            def att_high(p):
                act.wait_ge(S("av_ready"), 2 * p + 2)
                a.sig(A(yhi[:, ATT, p, :], bank(6 + p % 2)[:, 0:NA], ACT.Copy), "att_hi")

            for p in range(KT):
                feed(("q", p))
                if p:
                    softplus_part(2 * p - 2)
                    softplus_part(2 * p - 1)
                feed(("c", p))
                if p:
                    weights_of(2 * p - 2)
                    weights_of(2 * p - 1)
                feed(("h", p))
                if p:
                    att_high(p - 1)
                feed(("b", p))
                act.wait_ge(S("conv_y"), p + 1)
                a.sig(A(yhi[:, CONV, p, :], bb[:, p % 2, :], ACT.Copy), "conv_hi")
            softplus_part(14)
            softplus_part(15)
            feed(("gc", 0))
            weights_of(14)
            weights_of(15)
            feed(("ga", 0))
            att_high(KT - 1)
            for i in range(KT):
                for j, s in enumerate(("gc", "ga")):
                    if i:
                        feed((s, i))
                    act.wait_ge(S("gate_raw"), 2 * i + j + 1)
                    g_ = gate[:, (2 * i + j) % 4, :]
                    a.sig(A(g_, g_, ACT.Sigmoid, bias=pcol("b_gate", KT * j + i)), "gate_ready")
                feed(("pc", i))
                feed(("pa", i))
                act.wait_ge(S("merged_y"), i + 1)
                a.sig(A(yhi[:, MERGED, i, :], mm1[:, i % 2, :], ACT.Copy), "merged_hi")

            def out_squares(stage, n0, t0):
                for i in range(KT):
                    feed((stage, i))
                    act.wait_ge(S("mout_ready"), n0 + i + 1)
                    a.sig(A(sq[:, i, t0:T], mout[:, i, t0:T], ACT.Square), "sq_ready")

            out_squares("wo", 0, TA)
            exp_and_ln()
            inverse_rms(rpost[:, TA:T], NA, D, 2)
            x_high(1, "g_pre_ffn", TA, 0)
            inverse_rms(rinv[:, TA:T], NA, D, 3)
            for i in range(FT):
                feed(("fu", i))
                act.wait_ge(S("u_ready"), i + 1)
                a.sig(A(fcv[:, i % 2, :], fu[:, i % 2, 0:L], ACT.Copy, scale=pcol("conv_ffn", i)), "tap_ready")
                feed(("fg", i))
                act.wait_ge(S("u_conv"), i + 1)
                need(act, "ffn_y", i - 1)
                a.sig(A(fgl[:, i % 2, :], fcv[:, i % 2, :], ACT.Gelu_apprx_tanh), "gelu_ready")
                act.wait_ge(S("ffn_y"), i + 1)
                a.sig(A(fhi[:, i, :], fy[:, i % 2, :], ACT.Copy), "ffn_hi")
            out_squares("fd", KT, META)
            exp_and_ln()
            inverse_rms(rpost[:, META:T], L, D, 4)
            x_high(2, "even_norm", META, KT)
            inverse_rms(rinv[:, META:T], L, D, 5)

            for n, tile in enumerate([("eb", 0), ("ec", 0)] + [("ex", i) for i in range(KT)]):
                feed(tile)
                act.wait_ge(S("xconv"), n + 1)
                src = cvo[:, n % 2, :]
                if n == 0:
                    a.sig(A(bT, src, ACT.Silu), "xsilu")
                elif n == 1:
                    act.wait_ge(S("zeroed"), 6)
                    for g_ in range(2):
                        r = slice(64 * g_, 64 * g_ + 64)
                        (a.sig(A(cT[r, g_, :], cvo[r, n % 2, :], ACT.Silu), "xsilu") if g_
                         else a.step(A(cT[r, g_, :], cvo[r, n % 2, :], ACT.Silu)))
                else:
                    a.sig(A(xs[:, n - 2, :], src, ACT.Silu), "xsilu")
            feed(("es", 0))
            exp_and_ln()
            act.wait_ge(S("small_ready"), 1)
            a.step(A(small1[0:16, :], sm[0:16, :], ACT.Abs, bias=pcol("dt_bias")[0:16]))
            a.step(A(acol[0:16, 0:1], pcol("a_log")[0:16], ACT.Exp))
            a.settle()
            a.step(A(small1[0:16, :], small1[0:16, :], ACT.Exp, scale=-1.0))
            a.settle()
            a.sig(A(small1[0:16, :], small1[0:16, :], ACT.Ln, bias=one[0:16]), "dt_ln")
            for i in range(4):
                feed(("eq", i))
                act.wait_ge(S("lowrank"), i + 1)
                need(act, "decay_sum", i - 1)
                a.settle()
                b_ = bank(4 + i % 2)[:, 0:L]
                a.step(A(gtmp[:, i % 2, :], b_, ACT.Abs, bias=pcol("gate_b", i)))
                a.settle()
                a.step(A(gtmp[:, i % 2, :], gtmp[:, i % 2, :], ACT.Exp, scale=-1.0))
                a.settle()
                a.sig(A(gtmp[:, i % 2, :], gtmp[:, i % 2, :], ACT.Ln, bias=one), "gate_ln")
            act.wait_ge(S("acs_ready"), 1)
            act.dma_start(scratch, acs[0:16, :]).then_inc(S("bc_out"), 16)
            act.wait_ge(S("bc_out"), 16)

            def spread(i):
                act.dma_start(bc[:, i % 2], scratch[2 * i:2 * i + 2, :].rearrange("(o h) t -> o h t", o=1)
                              .partition_broadcast(P)).then_inc(S(f"spread{i % 2}"), 16)

            for i in range(4):
                feed(("ek", i))
            for i in range(4):
                feed(("ev", i))

            def silu_part(n, dst):
                act.wait_ge(S("z_half"), n + 1)
                a.sig(A(cvo[:, n % 2, :], dst, ACT.Tanh), "z_tanh")

            act.wait_ge(S("xd_ready"), 4)
            act.wait_ge(S("decay_sum"), 4)
            spread(0)
            spread(1)
            for i in range(KT):
                feed(("ez", i))
                silu_part(2 * i, zs[:, i % 2, :])
                feed(("eg", i))
                silu_part(2 * i + 1, gs[:, i, :])
                for h in (2 * i, 2 * i + 1):
                    act.wait_ge(S("decay_arg"), h + 1)
                    a.sig(A(dec[:, h % 2, :], dec[:, h % 2, :], ACT.Exp), "decay_exp")
                if i + 2 < KT:
                    spread(i + 2)
                act.wait_ge(S("yz_ready"), i + 1)
                need(act, "sum_part", i - 1)
                a.sig(A(sqy[:, i % 2, :], xs[:, i, :], ACT.Square), "sqy_ready")
            exp_and_ln()
            inverse_rms(rpost[:, 0:L], L, D, 6)
            for i in range(KT):
                act.wait_ge(S("yn_ready"), i + 1)
                a.sig(A(ehi[:, i, :], xs[:, i, :], ACT.Copy), "e_hi")

            def gla_exps(p):
                act.wait_ge(S("gla_arg"), 2 * p + 2)
                need(act, "gla_qk", p)
                k = p % 2
                a.step(A(em, ka[:, k, :], ACT.Exp, scale=1.0 / 16))
                a.step(A(kb[:, k, :], kb[:, k, :], ACT.Exp, scale=1.0 / 16))
                a.settle()
                a.step(A(ka[:, k, :], ka[:, k, :], ACT.Exp, scale=-1.0 / 16))
                need(act, "st_ready", p - 1)
                a.sig(A(eg[:, k, :], gcs[:, p, :], ACT.Exp, scale=1.0 / 16), "gla_exp")

            gla_exps(0)
            for p in range(4):
                if p < 3:
                    gla_exps(p + 1)
                act.wait_ge(S("gla_o"), p + 1)
                need(act, "gla_og", 2 * p)
                a.settle()
                a.sig(A(osq, bank(4 + p % 2), ACT.Square), "gla_sq")
                act.wait_ge(S("gla_sums"), p + 1)
                a.settle()
                a.step(A(orv, bank(0), ACT.Ln, scale=1.0 / P, bias=epsb))
                a.settle()
                a.sig(A(orv, orv, ACT.Exp, scale=-0.5), "gla_rms")
                for hh in range(2):
                    act.wait_ge(S("gla_og"), 2 * p + hh + 1)
                    a.sig(A(ehi[:, KT + 2 * p + hh, :], gs[:, 2 * p + hh, :], ACT.Copy), "e_hi")
            for i in range(KT):
                feed(("eo", i))
            x_high(3, "odd_norm", META, 2 * KT)
            inverse_rms(rinv[:, META:T], L, D, 7)
            for i in range(KT):
                feed(("mk", i))
            for i in range(4):
                feed(("mv", i))

            def soft_exp(h):
                act.wait_ge(S("m_max"), h + 1)
                need(act, "p_T", h - 1)
                a.sig(A(pr[:, h % 2, 0:P], ssm[:, h % 2, 0:P], ACT.Exp, bias=mst[:, h % 2, 0:1],
                        accum_out=mst[:, h % 2, 2:3]), "m_exp")
                a.sig(A(pr[:, h % 2, P:CC], ssm[:, h % 2, P:CC], ACT.Exp, bias=mst[:, h % 2, 1:2],
                        accum_out=mst[:, h % 2, 3:4]), "m_exp")

            def prob_copy(h):
                act.wait_ge(S("p_T"), h + 1)
                need(act, "m_av", h - 1)
                a.sig(A(prT[:, h % 2, :], bank(6)[:, 0:CC], ACT.Copy), "p_taken")

            for i in range(KT + 1):
                if i < KT:
                    feed(("mq", i))
                if i:
                    soft_exp(2 * i - 2)
                    soft_exp(2 * i - 1)
                if i < KT:
                    feed(("mz", i))
                    act.wait_ge(S("mz_half"), i + 1)
                    a.sig(A(mzs[:, i % 2, :], mz[:, i % 2, :], ACT.Tanh), "mz_tanh")
                if i:
                    prob_copy(2 * i - 2)
                    prob_copy(2 * i - 1)
                    act.wait_ge(S("mo_ready"), i)
                    a.sig(A(ehi[:, i - 1, :], mo[:, (i - 1) % 2, :], ACT.Copy), "mo_hi")
            for i in range(KT):
                feed(("mo", i))
            for i in range(KT):
                act.wait_ge(S("h_ready"), 3 * KT + i + 1)
                a.sig(A(sq[:, i, META:T], H[:, i, META:T], ACT.Square), "sq_ready")
            exp_and_ln()
            inverse_rms(rinv[:, META:T], L, D, 8)
            for i in range(KT):
                act.wait_ge(S("final"), i + 1)
                act.dma_start(out[:, i, :], mout[:, i, 0:L]).then_inc(S("stored"), 16)
            act.wait_ge(S("stored"), 16 * KT)

        @block.vector
        def _(dve):
            d = Steps(dve, "dve_step")
            V = nc.vector
            nxt = [0]
            TT, STT, TS = V.tensor_tensor, V.scalar_tensor_tensor, V.tensor_scalar

            def split_lo():
                c = nxt[0]
                nxt[0] += 1
                if c >= NCHUNKS:
                    return
                dve.wait_ge(S("hi_ready"), c + 1)
                s = c % RING
                d.sig(TT(wlo[:, s * CW:(s + 1) * CW], raw[:, (c % RAW) * CW:(c % RAW + 1) * CW],
                         whi[:, s * CW:(s + 1) * CW].bitcast(F32), ALU.subtract), "lo_ready")

            def feed(tile):
                for _ in chunk_of(tile):
                    split_lo()

            def result(tile, o=0, width=NA):
                n = FIRST_OUT[tile] + o
                dve.wait_ge(S("out_ready"), n + 1)
                return bank(n % 4)[:, 0:width]

            def x_low(gain, t0, base):
                for kt in range(KT):
                    dve.wait_ge(S("x_hi"), base + kt + 1)
                    d.sig(STT(out=xlo[:, kt, t0:T], in0=H[:, kt, t0:T], scalar=pcol(gain, kt),
                              in1=xhi[:, kt, t0:T].bitcast(F32), op0=ALU.mult, op1=ALU.subtract), "x_split")

            dve.wait_ge(S("load_params"), 16)
            dve.wait_ge(S("load_x"), 16)
            dve.wait_ge(S("load_masks"), 16)
            for _ in range(2):
                split_lo()
            x_low("g_pre_mix", 0, 0)
            for _ in range(RING - 2):
                split_lo()
            dve.wait_ge(S("rms_ready"), 1)
            for i in range(KT):
                r = result(("k", i), 0, T)
                d.sig(TT(keysT[:, i, 0:T], r, rinv[:, 0:T], ALU.mult), "out_taken")
                feed(("k", i))
            dve.wait_ge(S("rinv_T"), 1)
            d.step(V.tensor_copy(rcol[:, 0:1], bank(6)[:, 0:1]))
            d.step(V.tensor_copy(rcol[:, 1:2], bank(6)[:, P:P + 1]))
            d.step(V.tensor_copy(rcol[0:T - L, 2:3], bank(6)[0:T - L, 2 * P:2 * P + 1]))
            d.settle()
            dve.wait_ge(S("zeroed"), 3)
            for i in range(4):
                for o in range(3):
                    n = P if o < 2 else T - L
                    r = result(("v", i), o, L)
                    d.sig(TS(vals[0:n, o, 256 * i:256 * i + 256], r[0:n], rcol[0:n, o:o + 1], None, ALU.mult),
                          "out_taken")
                feed(("v", i))

            def fail(h):
                dve.wait_ge(S("sp_ready"), h + 1)
                need(dve, "a_ready", h - 1)
                d.settle()
                d.step(STT(out=fz[:, h % 2, :], in0=bank(4 + h % 2)[:, 0:ZC], scalar=0.0, in1=sp[:, h % 2, :],
                           op0=ALU.max, op1=ALU.add))
                d.settle()
                d.sig(TT(fz[:, h % 2, :], fz[:, h % 2, :], mask("stick"), ALU.mult), "f_ready")

            def log_weight(h):
                dve.wait_ge(S("loga_ready"), h + 1)
                d.settle()
                d.sig(STT(out=fz[:, h % 2, :], in0=bank(4 + h % 2)[:, 0:ZC], scalar=0.0, in1=mask("stick_neg"),
                          op0=ALU.min, op1=ALU.add), "loga_taken")

            def att_low(p):
                dve.wait_ge(S("att_hi"), p + 1)
                d.sig(TT(ylo[:, ATT, p, :], bank(6 + p % 2)[:, 0:NA], yhi[:, ATT, p, :].bitcast(F32), ALU.subtract),
                      "att_split")

            def conv_low(p):
                dve.wait_ge(S("conv_hi"), p + 1)
                d.sig(TT(ylo[:, CONV, p, :], bb[:, p % 2, :], yhi[:, CONV, p, :].bitcast(F32), ALU.subtract),
                      "conv_split")

            for p in range(KT):
                r = result(("q", p), 0, NA)
                need(dve, "z_ready", 2 * p - 2)
                d.settle()
                for e in range(2):
                    rows = slice(64 * e, 64 * e + 64)
                    ins = STT(out=qpair[rows, p % 2, e, TA:T], in0=r[rows], scalar=0.125, in1=rinv[rows, TA:T],
                              op0=ALU.mult, op1=ALU.mult)
                    d.sig(ins, "out_taken") if e else d.step(ins)
                feed(("q", p))
                if p:
                    fail(2 * p - 2)
                    fail(2 * p - 1)
                r = result(("c", p), 0, T - TC)
                d.settle()
                d.sig(TT(cbuf[:, p % 2, TC:T], r, rinv[:, TC:T], ALU.mult), "out_taken")
                feed(("c", p))
                if p:
                    log_weight(2 * p - 2)
                    log_weight(2 * p - 1)
                r = result(("h", p), 0, T - TC)
                ch = chbuf[:, p % 2, :]
                d.settle()
                d.sig(TT(ch[:, TC:T], r, rinv[:, TC:T], ALU.mult), "out_taken")
                d.settle()
                d.step(TT(ch[:, TC:T], ch[:, TC:T], cbuf[:, p % 2, TC:T], ALU.mult))
                d.settle()
                c_ = cv[:, p % 2, :]
                d.step(TS(c_, ch[:, TC:T - 2], pcol("conv_mix", p), None, ALU.mult))
                for j in (1, 2):
                    d.settle()
                    d.step(STT(out=c_, in0=ch[:, TC + j:T - 2 + j], scalar=pcol("conv_mix", KT * j + p), in1=c_,
                               op0=ALU.mult, op1=ALU.add))
                feed(("h", p))
                if p:
                    att_low(p - 1)
                r = result(("b", p), 0, NA)
                if p:
                    conv_low(p - 1)
                d.settle()
                d.sig(TT(bb[:, p % 2, :], r, rinv[:, TA:T], ALU.mult), "out_taken")
                d.settle()
                d.sig(TT(bb[:, p % 2, :], bb[:, p % 2, :], c_, ALU.mult), "conv_y")
                feed(("b", p))
            conv_low(KT - 1)
            fail(14)
            fail(15)

            def gate_raw(s, i, j):
                r = result((s, i), 0, NA)
                d.settle()
                d.sig(TT(gate[:, (2 * i + j) % 4, :], r, rinv[:, TA:T], ALU.mult), "gate_raw")
                feed((s, i))

            gate_raw("gc", 0, 0)
            log_weight(14)
            log_weight(15)
            gate_raw("ga", 0, 1)
            att_low(KT - 1)
            for i in range(KT):
                if i:
                    gate_raw("gc", i, 0)
                    gate_raw("ga", i, 1)
                m1 = mm1[:, i % 2, :]
                r = result(("pc", i), 0, NA)
                dve.wait_ge(S("gate_ready"), 2 * i + 1)
                d.settle()
                d.step(TT(m1, r, gate[:, (2 * i) % 4, :], ALU.mult))
                feed(("pc", i))
                r = result(("pa", i), 0, NA)
                dve.wait_ge(S("gate_ready"), 2 * i + 2)
                g2 = gate[:, (2 * i + 1) % 4, :]
                d.settle()
                d.step(TT(g2, r, g2, ALU.mult))
                d.settle()
                d.sig(TT(m1, m1, g2, ALU.add), "merged_y")
                feed(("pa", i))
                dve.wait_ge(S("merged_hi"), i + 1)
                d.sig(TT(ylo[:, MERGED, i, :], m1, yhi[:, MERGED, i, :].bitcast(F32), ALU.subtract), "merged_split")

            def out_tiles(stage, t0):
                for i in range(KT):
                    r = result((stage, i), 0, T - t0)
                    d.sig(V.tensor_copy(mout[:, i, t0:T], r), "mout_ready")
                    feed((stage, i))

            def post_norm(nth, gain_post, gain_pre, base, t0):
                dve.wait_ge(S("rms_ready"), nth)
                d.settle()

                def low(kt):
                    dve.wait_ge(S("x_hi"), base + kt + 1)
                    d.sig(STT(out=xlo[:, kt, t0:T], in0=H[:, kt, t0:T], scalar=pcol(gain_pre, kt),
                              in1=xhi[:, kt, t0:T].bitcast(F32), op0=ALU.mult, op1=ALU.subtract), "x_split")

                for kt in range(KT):
                    m = mout[:, kt, t0:T]
                    d.step(STT(out=m, in0=m, scalar=pcol(gain_post, kt), in1=rpost[:, t0:T], op0=ALU.mult, op1=ALU.mult))
                    d.settle()
                    d.sig(TT(H[:, kt, t0:T], H[:, kt, t0:T], m, ALU.add), "h_ready")
                    if kt:
                        low(kt - 1)
                low(KT - 1)

            out_tiles("wo", TA)
            post_norm(2, "g_post_mix", "g_pre_ffn", KT, TA)
            dve.wait_ge(S("rms_ready"), 3)
            for i in range(FT):
                u, c_ = fu[:, i % 2, :], fcv[:, i % 2, :]
                r = result(("fu", i), 0, NA)
                need(dve, "tap_ready", i - 1)
                d.settle()
                d.sig(TT(u, r, rinv[:, TA:T], ALU.mult), "u_ready")
                feed(("fu", i))
                dve.wait_ge(S("tap_ready"), i + 1)
                for j in (1, 2):
                    d.settle()
                    ins = STT(out=c_, in0=u[:, j:L + j], scalar=pcol("conv_ffn", FT * j + i), in1=c_,
                              op0=ALU.mult, op1=ALU.add)
                    d.sig(ins, "u_conv") if j == 2 else d.step(ins)
                r = result(("fg", i), 0, L)
                dve.wait_ge(S("gelu_scaled"), i + 1)
                need(dve, "ffn_split", i - 1)
                d.sig(TT(fy[:, i % 2, :], r, fgl[:, i % 2, :], ALU.mult), "ffn_y")
                feed(("fg", i))
            out_tiles("fd", META)
            post_norm(4, "g_post_ffn", "even_norm", 2 * KT, META)
            dve.wait_ge(S("rms_ready"), 5)
            rL = rinv[:, META:T]

            dve.wait_ge(S("zeroed"), 6)
            for n, (tile, ct) in enumerate([(("eb", 0), 8), (("ec", 0), 9)] + [(("ex", i), i) for i in range(KT)]):
                r = result(tile, 0, L)
                s_, c_ = scr2[:, n % 2, :], cvo[:, n % 2, :]
                need(dve, "xsilu", n - 1)
                d.settle()
                d.sig(TT(s_[:, 3:3 + L], r, rL, ALU.mult), "out_taken")
                d.settle()
                d.step(TS(c_, s_[:, 0:L], pcol("even_conv", ct), pcol("even_conv_b", ct), ALU.mult, ALU.add))
                for j in (1, 2, 3):
                    d.settle()
                    ins = STT(out=c_, in0=s_[:, j:L + j], scalar=pcol("even_conv", 10 * j + ct), in1=c_,
                              op0=ALU.mult, op1=ALU.add)
                    d.sig(ins, "xconv") if j == 3 else d.step(ins)
                feed(tile)
            r = result(("es", 0), 0, L)
            d.settle()
            d.sig(TT(sm, r, rL, ALU.mult), "small_ready")
            feed(("es", 0))
            d.settle()
            d.step(TS(small2[0:16, :], sm[0:16, :], pcol("dt_bias")[0:16], 0.0, ALU.add, ALU.max))
            dve.wait_ge(S("dt_ln"), 1)
            d.settle()
            d.step(TT(scans[0:16, :], small2[0:16, :], small1[0:16, :], ALU.add))
            d.step(TS(acol[0:16, 1:2], acol[0:16, 0:1], -1.0, None, ALU.mult))
            d.settle()
            d.step(TS(small2[0:16, :], scans[0:16, :], acol[0:16, 1:2], None, ALU.mult))
            d.settle()
            d.sig(V.tensor_tensor_scan(acs[0:16, :], mask("ones")[0:16, 0:L], small2[0:16, :], 0.0, ALU.mult, ALU.add),
                  "acs_ready")
            d.settle()
            d.sig(V.tensor_copy(scans[LR_ROW:LR_ROW + 16, :], acs[0:16, :]), "scans_ready")
            for i in range(4):
                r = result(("eq", i), 0, L)
                d.sig(STT(out=e_q[:, i, :], in0=r, scalar=0.125, in1=rL, op0=ALU.mult, op1=ALU.mult), "out_taken")
                feed(("eq", i))
                dve.wait_ge(S("gate_ln"), i + 1)
                d.settle()
                d.step(TS(small2, bank(4 + i % 2)[:, 0:L], pcol("gate_b", i), 0.0, ALU.add, ALU.min))
                d.settle()
                d.step(TT(small2, small2, gtmp[:, i % 2, :], ALU.subtract))
                d.settle()
                d.sig(V.tensor_tensor_scan(gcs[:, i, :], mask("restart"), small2, 0.0, ALU.mult, ALU.add), "decay_sum")
            for i in range(4):
                r = result(("ek", i), 0, L)
                d.sig(TT(e_k[:, i, :], r, rL, ALU.mult), "out_taken")
                feed(("ek", i))
            dve.wait_ge(S("rinv_T"), 2)
            d.settle()
            d.step(V.tensor_copy(rcol[:, 0:1], bank(6)[:, 0:1]))
            d.step(V.tensor_copy(rcol[:, 1:2], bank(6)[:, P:P + 1]))
            d.sig(V.tensor_copy(tkc, bank(6)[:, 256:512].rearrange("p (a b) -> p a b", a=2)), "tkc_ready")
            for g_ in range(2):
                dve.wait_ge(S("cb_ready"), g_ + 1)
                d.sig(TT(cb[:, g_, :], bank(4 + g_)[:, 0:CC], mask("causal"), ALU.mult), "cb_taken")
            d.settle()
            for t in range(2):
                for q in range(2):
                    dve.wait_ge(S("xT_ready"), 2 * t + q + 1)
                    src = bank(4 + q).rearrange("p (h c) -> p h c", c=64)
                    dst = xd[:, t, 512 * q:512 * q + 512].rearrange("p (h c) -> p h c", c=64)
                    dtv = tkc[:, t, 8 * q:8 * q + 8].unsqueeze(2).to_broadcast([P, 8, 64])
                    d.sig(TT(dst, src, dtv, ALU.mult), "xd_ready")
            for i in range(4):
                for o in range(2):
                    r = result(("ev", i), o, L)
                    d.sig(TS(vb[:, o, 256 * i:256 * i + 256], r, rcol[:, o:o + 1], None, ALU.mult), "out_taken")
                feed(("ev", i))

            def z_half(n, tile, dst):
                r = result(tile, 0, L)
                d.sig(STT(out=dst, in0=r, scalar=0.5, in1=rL, op0=ALU.mult, op1=ALU.mult), "z_half")
                feed(tile)

            def z_full(n, dst):
                dve.wait_ge(S("z_tanh"), n + 1)
                d.settle()
                d.step(STT(out=dst, in0=cvo[:, n % 2, :], scalar=1.0, in1=dst, op0=ALU.add, op1=ALU.mult))

            for i in range(KT):
                d.settle()
                z_half(2 * i, ("ez", i), zs[:, i % 2, :])
                z_half(2 * i + 1, ("eg", i), gs[:, i, :])
                dve.wait_ge(S(f"spread{i % 2}"), 16 * (i // 2 + 1))
                for h in (2 * i, 2 * i + 1):
                    need(dve, "y_ready", h - 1)
                    d.settle()
                    for t in range(2):
                        w_ = slice(0, L) if t == 0 else slice(L, CC)
                        ins = TS(dec[:, h % 2, w_], bc[:, i % 2, h % 2, P * t:L], tkc[:, t, LR_ROW + h:LR_ROW + h + 1], 0.0,
                                 ALU.subtract, ALU.min)
                        d.sig(ins, "decay_arg") if t else d.step(ins)
                z_full(2 * i, zs[:, i % 2, :])
                z_full(2 * i + 1, gs[:, i, :])
                for h in (2 * i, 2 * i + 1):
                    dve.wait_ge(S("decay_exp"), h + 1)
                    d.sig(TT(dec[:, h % 2, :], dec[:, h % 2, :], cb[:, h // 8, :], ALU.mult), "m_ready")
                dve.wait_ge(S("y_ready"), 2 * i + 2)
                d.settle()
                d.sig(STT(out=xs[:, i, :], in0=xs[:, i, :], scalar=pcol("d_skip", i), in1=bank(4 + i % 2)[:, 0:L],
                          op0=ALU.mult, op1=ALU.add), "ssd_y")
                d.settle()
                d.sig(TT(xs[:, i, :], xs[:, i, :], zs[:, i % 2, :], ALU.mult), "yz_ready")
            def gla_args(p):
                need(dve, "gla_o", p - 1)
                gv = gcs[:, p, :].rearrange("p (c t) -> p c t", t=64)
                d.settle()
                d.sig(TT(ka[:, p % 2, :].rearrange("p (c t) -> p c t", t=64), gv,
                         gv[:, :, 32:33].to_broadcast([P, 4, 64]), ALU.subtract), "gla_arg")
                d.sig(TT(kb[:, p % 2, :].rearrange("p (c t) -> p c t", t=64), gv[:, :, 63:64].to_broadcast([P, 4, 64]),
                         gv, ALU.subtract), "gla_arg")

            dve.wait_ge(S("rms_ready"), 6)
            d.settle()
            for i in range(KT):
                d.sig(STT(out=xs[:, i, :], in0=xs[:, i, :], scalar=pcol("ssd_norm", i), in1=rpost[:, 0:L],
                          op0=ALU.mult, op1=ALU.mult), "yn_ready")
            for i in range(KT):
                dve.wait_ge(S("e_hi"), i + 1)
                d.sig(TT(elo[:, i, :], xs[:, i, :], ehi[:, i, :].bitcast(F32), ALU.subtract), "e_split")
            dve.wait_ge(S("zeroed"), 9)
            gla_args(0)
            for p in range(4):
                k = p % 2
                if p < 3:
                    gla_args(p + 1)
                dve.wait_ge(S("gla_exp"), p + 1)
                d.sig(TT(kb[:, k, :], kb[:, k, :], e_k[:, p, :], ALU.mult), "gla_kl")
                d.step(TT(ka[:, k, :], ka[:, k, :], e_k[:, p, :], ALU.mult))
                for e in range(2):
                    rows = slice(64 * e, 64 * e + 64)
                    d.step(TT(qg[rows, k, e, :], eg[rows, k, :], e_q[rows, p, :], ALU.mult))
                    ins = TT(qe[rows, k, e, :], em[rows], e_q[rows, p, :], ALU.mult)
                    d.sig(ins, "gla_qk") if e else d.step(ins)
                dve.wait_ge(S("klT_ready"), p + 1)
                d.sig(V.tensor_copy(klt[:, k].rearrange("p a b -> p (a b)"), bank(1)[:, 0:L]), "klt_ready")
                dve.wait_ge(S("kv_ready"), p + 1)
                need(dve, "gla_o", p)
                kv = [bank(6 + n % 2)[:, P * n:P * n + P] for n in range(3)]
                d.settle()
                d.step(V.tensor_copy(st[:, 0, :], kv[0]))
                for n in (1, 2):
                    d.settle()
                    ins = STT(out=st[:, n, :], in0=st[:, n - 1, :], scalar=eg[:, k, 64 * n + 63:64 * n + 64],
                              in1=kv[n], op0=ALU.mult, op1=ALU.add)
                    d.sig(ins, "st_ready") if n == 2 else d.step(ins)
                for t in range(2):
                    dve.wait_ge(S("sc_ready"), 2 * p + t + 1)
                    d.settle()
                    d.sig(V.copy_predicated(sc[:, t, :], mask("chunk").bitcast(I32), bank(2 + t)[:, 0:L]), "sc_taken")
                dve.wait_ge(S("gla_rms"), p + 1)
                d.settle()
                for hh in range(2):
                    w_ = slice(L * hh, L * hh + L)
                    ins = STT(out=osq[:, w_], in0=bank(4 + p % 2)[:, w_], scalar=pcol("gla_norm"), in1=orv[:, w_],
                              op0=ALU.mult, op1=ALU.mult)
                    d.sig(ins, "gla_on") if hh else d.step(ins)
                d.settle()
                for hh in range(2):
                    d.sig(TT(gs[:, 2 * p + hh, :], gs[:, 2 * p + hh, :], osq[:, L * hh:L * hh + L], ALU.mult), "gla_og")
                for hh in range(2):
                    dve.wait_ge(S("e_hi"), KT + 2 * p + hh + 1)
                    d.sig(TT(elo[:, KT + 2 * p + hh, :], gs[:, 2 * p + hh, :],
                             ehi[:, KT + 2 * p + hh, :].bitcast(F32), ALU.subtract), "e_split")

            def residual(stage, gain, base):
                for i in range(KT):
                    r = result((stage, i), 0, L)
                    d.sig(TT(H[:, i, META:T], r, H[:, i, META:T], ALU.add), "h_ready")
                    feed((stage, i))

            residual("eo", None, None)
            x_low("odd_norm", META, 3 * KT)
            dve.wait_ge(S("rms_ready"), 7)
            d.settle()
            for i in range(KT):
                r = result(("mk", i), 0, L)
                d.sig(TT(mkT[:, i, :], r, rL, ALU.mult), "out_taken")
                feed(("mk", i))
            dve.wait_ge(S("rinv_T"), 3)
            d.step(V.tensor_copy(rcol[:, 0:1], bank(6)[:, 0:1]))
            d.sig(V.tensor_copy(rcol[:, 1:2], bank(6)[:, P:P + 1]), "rcol3")
            d.settle()
            for i in range(4):
                for o in range(2):
                    r = result(("mv", i), o, L)
                    d.sig(TS(mval[:, o, 256 * i:256 * i + 256], r, rcol[:, o:o + 1], None, ALU.mult), "out_taken")
                feed(("mv", i))
            dve.wait_ge(S("zeroed"), 10)

            def scores_max(h):
                s_ = ssm[:, h % 2, :]
                dve.wait_ge(S("s_ready"), h + 1)
                need(dve, "m_exp", 2 * h - 2)
                d.settle()
                d.sig(TT(s_, bank(4 + h % 2)[:, 0:CC], mask("causal_neg"), ALU.add), "s_taken")
                d.settle()
                d.step(V.tensor_reduce(mst[:, h % 2, 4:5], s_[:, 0:P], AX_X, ALU.max))
                d.step(V.tensor_reduce(mst[:, h % 2, 5:6], s_[:, P:CC], AX_X, ALU.max))
                d.settle()
                d.sig(TS(mst[:, h % 2, 0:2], mst[:, h % 2, 4:6], -1.0, None, ALU.mult), "m_max")

            def normalise(h):
                dve.wait_ge(S("m_exp"), 2 * h + 2)
                d.settle()
                d.step(V.reciprocal(mst[:, h % 2, 6:8], mst[:, h % 2, 2:4]))
                d.settle()
                for t in range(2):
                    w_ = slice(0, P) if t == 0 else slice(P, CC)
                    ins = TS(pr[:, h % 2, w_], pr[:, h % 2, w_], mst[:, h % 2, 6 + t:7 + t], None, ALU.mult)
                    d.sig(ins, "p_ready") if t else d.step(ins)

            for i in range(KT + 1):
                if i < KT:
                    r = result(("mq", i), 0, L)
                    need(dve, "s_ready", 2 * i - 2)
                    d.settle()
                    for e in range(2):
                        rows = slice(64 * e, 64 * e + 64)
                        ins = STT(out=mqp[rows, i % 2, e, :], in0=r[rows], scalar=0.125, in1=rL[rows],
                                  op0=ALU.mult, op1=ALU.mult)
                        d.sig(ins, "out_taken") if e else d.step(ins)
                    feed(("mq", i))
                if i:
                    scores_max(2 * i - 2)
                    scores_max(2 * i - 1)
                if i < KT:
                    r = result(("mz", i), 0, L)
                    need(dve, "mz_tanh", i - 1)
                    d.settle()
                    d.sig(STT(out=mz[:, i % 2, :], in0=r, scalar=0.5, in1=rL, op0=ALU.mult, op1=ALU.mult), "mz_half")
                    feed(("mz", i))
                if i:
                    normalise(2 * i - 2)
                    normalise(2 * i - 1)
                    dve.wait_ge(S("m_av"), 2 * i)
                    need(dve, "mo_hi", i - 2)
                    d.settle()
                    j = i - 1
                    d.sig(TT(mo[:, j % 2, :], bank(7)[:, 0:L], mzs[:, j % 2, :], ALU.mult), "mo_ready")
                    dve.wait_ge(S("mo_hi"), i)
                    d.settle()
                    d.sig(TT(elo[:, j, :], mo[:, j % 2, :], ehi[:, j, :].bitcast(F32), ALU.subtract), "mo_split")
                if i < KT:
                    dve.wait_ge(S("mz_tanh"), i + 1)
                    d.settle()
                    d.step(STT(out=mzs[:, i % 2, :], in0=mzs[:, i % 2, :], scalar=1.0, in1=mz[:, i % 2, :],
                               op0=ALU.add, op1=ALU.mult))
            residual("mo", None, None)
            dve.wait_ge(S("rms_ready"), 8)
            d.settle()
            for i in range(KT):
                d.sig(STT(out=mout[:, i, 0:L], in0=H[:, i, META:T], scalar=pcol("final_norm", i), in1=rL,
                          op0=ALU.mult, op1=ALU.mult), "final")

        @block.tensor
        def _(pe):
            n_sig = {}
            mm, tr = nc.tensor.matmul, nc.tensor.transpose
            ident = mask("identity")
            ones = mask("ones")[:, 0:P]

            taken = {}
            cnt = {}
            for s_, i_, b_, n_ in STREAM:
                name = {"gc": "gate_raw", "ga": "gate_raw", "pc": None, "pa": "merged_y", "wo": "mout_ready",
                        "fd": "mout_ready", "fu": "u_ready", "fg": "ffn_y", "es": "small_ready", "ez": "z_half",
                        "eg": "z_half", "eo": "h_ready", "mo": "h_ready", "mz": "mz_half"}.get(s_, "out_taken")
                for o in range(n_):
                    if name is None:
                        taken[FIRST_OUT[s_, i_] + o] = ("merged_y", i_ + 1)
                        continue
                    if name == "h_ready" and s_ == "eo" and i_ == 0:
                        cnt[name] = 2 * KT
                    cnt[name] = cnt.get(name, 0) + 1
                    taken[FIRST_OUT[s_, i_] + o] = (name, cnt[name])

            def bank_free(n):
                if n >= 4:
                    pe.wait_ge(S(taken[n - 4][0]), taken[n - 4][1])

            def project(tile, hi, lo, a, b, ready=None, toks=None):
                f, nb, no = FIRST_BLOCK[tile], BLOCKS_OF[tile], FIRST_OUT[tile]
                for o in range(OUTS_OF[tile]):
                    bank_free(no + o)
                step = 1 if toks is None else 2
                for j in range(0, nb, step):
                    c, kt = (f + j) // BPC, j // step
                    at = (c % RING) * CW + ((f + j) % BPC) * P
                    if (f + j) % BPC == 0 or j == 0:
                        pe.wait_ge(S("lo_ready"), c + 1)
                    if ready is not None:
                        ready(kt)
                    first, last = j == 0, j + step >= nb
                    outs = [None] if toks is None else toks
                    for o, tok in enumerate(outs):
                        for n, (w_, x_) in enumerate(((whi, hi), (whi, lo), (wlo, hi))):
                            wt = w_[:, at:at + step * P]
                            s0, s1 = first and n == 0, last and n == 2
                            if tok is None:
                                ins = mm(bank(no % 4)[:, 0:b - a], wt, x_[:, kt, a:b], start=s0, stop=s1)
                            else:
                                t0, t1 = tok
                                ins = mm(bank((no + o) % 4)[0:t1 - t0, 0:2 * P], x_[:, kt, t0:t1], wt,
                                         start=s0, stop=s1)
                        if last:
                            ins.then_inc(S("out_ready"), 1)
                    if (f + j + step) % BPC == 0 and not last:
                        ins.then_inc(S("chunk_read"), 1)

            def sums(base, a, b, nth):
                for kt in range(KT):
                    pe.wait_ge(S("sq_ready"), base + kt + 1)
                    ins = mm(bank(SSB)[:, 0:b - a], ones, sq[:, kt, a:b], start=kt == 0, stop=kt == KT - 1)
                ins.then_inc(S("sums_ready"), 1)

            def x_ready(base):
                return lambda kt: pe.wait_ge(S("x_split"), base + kt + 1)

            def rinv_by_token(starts, nth):
                pe.wait_ge(S("rms_ready"), nth)
                for n, (t0, t1) in enumerate(starts):
                    ins = tr(bank(6)[0:t1 - t0, P * n:P * n + P], rinv[:, t0:t1], ident)
                return ins

            pe.wait_ge(S("load_masks"), 16)
            toks3 = [(0, P), (P, 2 * P), (2 * P, T)]
            toksL = [(META, META + P), (META + P, T)]
            project(("k", 0), xhi, xlo, 0, T, x_ready(0))
            sums(0, 0, T, 1)
            for i in range(1, KT):
                project(("k", i), xhi, xlo, 0, T)
            rinv_by_token(toks3, 1).then_inc(S("rinv_T"), 1)
            for i in range(4):
                project(("v", i), xhi, xlo, 0, T, toks=toks3)

            def scores(h):
                p, e = h // 2, h % 2
                if e == 0:
                    pe.wait_ge(S("out_taken"), Q_TAKEN[p])
                need(pe, "loga_taken", h - 1)
                for n, (c0, k0, t0) in enumerate(SEG):
                    ins = mm(bank(4 + e)[:, c0:c0 + T - t0], keysT[:, p, k0:k0 + P], qpair[:, p % 2, e, t0:T],
                             start=n == 0, stop=n == 2, skip_group_check=True)
                ins.then_inc(S("z_ready"), 1)

            def survive(h):
                pe.wait_ge(S("f_ready"), h + 1)
                zb, f_ = bank(4 + h % 2), fz[:, h % 2, :]
                later = mask("neg_ones")
                mm(zb[:, 0:ZC], mask("neg_tri"), f_, start=False, stop=False, skip_group_check=True)
                c1, c2 = SEG[1][0], SEG[2][0]
                mm(zb[:, 128 - TA:NA], later, f_[:, c1:c2], start=False, stop=False, skip_group_check=True)
                mm(zb[:, 256 - TA:NA], later, f_[:, c2:ZC], start=False, stop=False, skip_group_check=True)
                mm(zb[:, c1 + 128:c2], later, f_[:, c2:ZC], start=False, stop=True,
                   skip_group_check=True).then_inc(S("loga_ready"), 1)

            def attend(h):
                p, e = h // 2, h % 2
                pe.wait_ge(S("a_ready"), h + 1)
                need(pe, "att_split", p - 1)
                rows = slice(64 * e, 64 * e + 64)
                for n, (c0, k0, t0) in enumerate(SEG):
                    ins = mm(bank(6 + p % 2)[rows, t0 - TA:NA], vals[:, n, 64 * h:64 * h + 64],
                             aw[:, h % 2, c0:c0 + T - t0], start=n == 0, stop=n == 2, skip_group_check=True)
                ins.then_inc(S("av_ready"), 1)

            Q_TAKEN = [taken[FIRST_OUT["q", p]][1] for p in range(KT)]
            pe.wait_ge(S("zeroed"), 3)
            for p in range(KT):
                project(("q", p), xhi, xlo, TA, T)
                if p:
                    scores(2 * p - 2)
                    scores(2 * p - 1)
                project(("c", p), xhi, xlo, TC, T)
                if p:
                    survive(2 * p - 2)
                    survive(2 * p - 1)
                project(("h", p), xhi, xlo, TC, T)
                if p:
                    attend(2 * p - 2)
                    attend(2 * p - 1)
                project(("b", p), xhi, xlo, TA, T)
            scores(14)
            scores(15)
            project(("gc", 0), xhi, xlo, TA, T)
            survive(14)
            survive(15)
            project(("ga", 0), xhi, xlo, TA, T)
            attend(14)
            attend(15)
            for i in range(KT):
                if i:
                    project(("gc", i), xhi, xlo, TA, T)
                    project(("ga", i), xhi, xlo, TA, T)
                project(("pc", i), yhi[:, CONV], ylo[:, CONV], 0, NA,
                        (lambda kt: pe.wait_ge(S("conv_split"), kt + 1)) if i == 0 else None)
                project(("pa", i), yhi[:, ATT], ylo[:, ATT], 0, NA,
                        (lambda kt: pe.wait_ge(S("att_split"), kt + 1)) if i == 0 else None)

            def out_sums(base, i, t0):
                pe.wait_ge(S("sq_ready"), base + i + 1)
                ins = mm(bank(SSB)[:, 0:T - t0], ones, sq[:, i, t0:T], start=i == 0, stop=i == KT - 1)
                if i == KT - 1:
                    ins.then_inc(S("sums_ready"), 1)

            for i in range(KT):
                project(("wo", i), yhi[:, MERGED], ylo[:, MERGED], 0, NA,
                        (lambda kt: pe.wait_ge(S("merged_split"), kt + 1)) if i == 0 else None)
                if i:
                    out_sums(KT, i - 1, TA)
            out_sums(KT, KT - 1, TA)
            project(("fu", 0), xhi, xlo, TA, T, x_ready(KT))
            sums(2 * KT, TA, T, 3)
            for i in range(FT):
                if i:
                    project(("fu", i), xhi, xlo, TA, T)
                project(("fg", i), xhi, xlo, META, T)
            for i in range(KT):
                project(("fd", i), fhi, flo, 0, L,
                        (lambda kt: pe.wait_ge(S("ffn_split"), kt + 1)) if i == 0 else None)
                if i:
                    out_sums(3 * KT, i - 1, META)
            out_sums(3 * KT, KT - 1, META)

            project(("eb", 0), xhi, xlo, META, T, x_ready(2 * KT))
            sums(4 * KT, META, T, 5)
            project(("ec", 0), xhi, xlo, META, T)
            for i in range(KT):
                project(("ex", i), xhi, xlo, META, T)
            project(("es", 0), xhi, xlo, META, T)
            pe.wait_ge(S("load_gate"), 16)
            for i in range(4):
                pe.wait_ge(S("small_ready"), 1)
                need(pe, "decay_sum", i - 1)
                project(("eq", i), xhi, xlo, META, T)
                mm(bank(4 + i % 2)[:, 0:L], gw2[:, P * i:P * i + P], sm, start=True, stop=True).then_inc(S("lowrank"), 1)
            for i in range(4):
                project(("ek", i), xhi, xlo, META, T)
            rinv_by_token(toksL, 5)
            pe.wait_ge(S("scans_ready"), 1)
            for t in range(2):
                ins = tr(bank(6)[:, 256 + P * t:256 + P * t + P], scans[:, P * t:P * t + P], ident)
            ins.then_inc(S("rinv_T"), 1)
            pe.wait_ge(S("xsilu"), 2 + KT)
            pe.wait_ge(S("decay_sum"), 4)
            for g_ in range(2):
                for t in range(2):
                    ins = mm(bank(4 + g_)[:, (0, L)[t]:(L, CC)[t]], bT[:, P * t:P * t + P], cT[:, g_, P * t:L],
                             start=t == 0, stop=t == 1, skip_group_check=True)
                ins.then_inc(S("cb_ready"), 1)
            for t in range(2):
                for q in range(2):
                    if t == 0:
                        pe.wait_ge(S("cb_taken"), q + 1)
                    else:
                        pe.wait_ge(S("xd_ready"), q + 1)
                    for c in range(4):
                        ins = tr(bank(4 + q)[:, P * c:P * c + P], xs[:, 4 * q + c, P * t:P * t + P], ident)
                    ins.then_inc(S("xT_ready"), 1)
            for i in range(4):
                project(("ev", i), xhi, xlo, META, T, toks=toksL)
            pe.wait_ge(S("xd_ready"), 4)
            pe.wait_ge(S("tkc_ready"), 1)

            def ssd_head(h):
                i, e = h // 2, h % 2
                pe.wait_ge(S("m_ready"), h + 1)
                need(pe, "ssd_y", i - 1)
                rows = slice(64 * e, 64 * e + 64)
                for t in range(2):
                    ins = mm(bank(4 + i % 2)[rows, P * t:L], xd[:, t, 64 * h:64 * h + 64],
                             dec[:, h % 2, (0, L)[t]:(L, CC)[t]], start=t == 0, stop=t == 1, skip_group_check=True)
                ins.then_inc(S("y_ready"), 1)

            for i in range(KT):
                project(("ez", i), xhi, xlo, META, T)
                project(("eg", i), xhi, xlo, META, T)
                ssd_head(2 * i)
                ssd_head(2 * i + 1)
                pe.wait_ge(S("sqy_ready"), i + 1)
                mm(bank(SSB)[:, 0:L], ones, sqy[:, i % 2, :], start=i == 0, stop=i == KT - 1).then_inc(
                    S("sum_part") if i < KT - 1 else S("sums_ready"), 1)
            pe.wait_ge(S("z_half"), 2 * KT)
            for p in range(4):
                k = p % 2
                pe.wait_ge(S("gla_kl"), p + 1)
                need(pe, "klt_ready", p)
                for t in range(2):
                    ins = tr(bank(1)[:, P * t:P * t + P], kb[:, k, P * t:P * t + P], ident)
                ins.then_inc(S("klT_ready"), 1)
                pe.wait_ge(S("gla_qk"), p + 1)
                for t in range(2):
                    need(pe, "sc_taken", 2 * p + t - 1)
                    mm(bank(2 + t)[:, 0:L], ka[:, k, P * t:P * t + P], qe[:, k, :, P * t:P * t + P],
                       start=True, stop=True).then_inc(S("sc_ready"), 1)
                pe.wait_ge(S("klt_ready"), p + 1)
                need(pe, "st_ready", p)
                for n in range(3):
                    rows = slice(64 * (n % 2), 64 * (n % 2) + 64)
                    for e in range(2):
                        h = 2 * p + e
                        ins = mm(bank(6 + n % 2)[64 * e:64 * e + 64, P * n:P * n + P], klt[rows, k, n // 2, 64 * e:64 * e + 64],
                                 vb[rows, n // 2, P * h:P * h + P], start=True, stop=True, skip_group_check=True)
                ins.then_inc(S("kv_ready"), 1)
                ob = bank(4 + p % 2).rearrange("p (e t) -> p e t", e=2)
                need(pe, "gla_on", p - 1)
                first = True
                for t in range(2):
                    pe.wait_ge(S("sc_taken"), 2 * p + t + 1)
                    for e in range(2):
                        h = 2 * p + e
                        ins = mm(ob[:, e, P * t:P * t + P], vb[:, t, P * h:P * h + P], sc[:, t, P * e:P * e + P],
                                 start=first, stop=False, skip_group_check=True)
                        first = False
                pe.wait_ge(S("st_ready"), p + 1)
                for n in (1, 2, 3):
                    ins = mm(ob[:, :, 64 * n:64 * n + 64], st[:, n - 1, :], qg[:, k, :, 64 * n:64 * n + 64],
                             start=False, stop=n == 3, skip_group_check=True)
                ins.then_inc(S("gla_o"), 1)
                pe.wait_ge(S("gla_sq"), p + 1)
                mm(bank(0), ones, osq, start=True, stop=True).then_inc(S("gla_sums"), 1)
            pe.wait_ge(S("gla_rms"), 4)
            for i in range(KT):
                project(("eo", i), ehi, elo, 0, L,
                        (lambda kt: pe.wait_ge(S("e_split"), kt + 1)) if i == 0 else None)
            project(("mk", 0), xhi, xlo, META, T, x_ready(3 * KT))
            sums(5 * KT, META, T, 7)
            for i in range(1, KT):
                project(("mk", i), xhi, xlo, META, T)
            rinv_by_token(toksL, 7).then_inc(S("rinv_T"), 1)
            for i in range(4):
                project(("mv", i), xhi, xlo, META, T, toks=toksL)
            pe.wait_ge(S("rcol3"), 1)
            MQ = [taken[FIRST_OUT["mq", p]][1] for p in range(KT)]

            def m_scores(h):
                i, e = h // 2, h % 2
                if e == 0:
                    pe.wait_ge(S("out_taken"), MQ[i])
                need(pe, "s_taken", h - 1)
                for t in range(2):
                    ins = mm(bank(4 + e)[:, (0, P)[t]:(P, CC)[t]], mqp[:, i % 2, e, P * t:P * t + P],
                             mkT[:, i, 0:P * (t + 1)], start=t == 0, stop=t == 1, skip_group_check=True)
                ins.then_inc(S("s_ready"), 1)

            def m_turn(h):
                pe.wait_ge(S("p_ready"), h + 1)
                need(pe, "p_taken", h)
                for n in range(3):
                    ins = tr(bank(6)[:, P * n:P * n + P], pr[:, h % 2, P * n:P * n + P], ident)
                ins.then_inc(S("p_T"), 1)

            def m_attend(h):
                i, e = h // 2, h % 2
                pe.wait_ge(S("p_taken"), h + 1)
                if e == 0:
                    need(pe, "mo_ready", i)
                rows = slice(64 * e, 64 * e + 64)
                b_ = bank(7)
                mm(b_[rows, 0:L], mval[:, 0, 64 * h:64 * h + 64], prT[:, h % 2, 0:L], start=True, stop=False,
                   skip_group_check=True)
                mm(b_[rows, P:L], mval[:, 1, 64 * h:64 * h + 64], prT[:, h % 2, L:CC], start=False, stop=True,
                   skip_group_check=True).then_inc(S("m_av"), 1)

            pe.wait_ge(S("zeroed"), 10)
            for i in range(KT + 1):
                if i < KT:
                    project(("mq", i), xhi, xlo, META, T)
                if i:
                    m_scores(2 * i - 2)
                    m_scores(2 * i - 1)
                if i < KT:
                    project(("mz", i), xhi, xlo, META, T)
                if i:
                    m_turn(2 * i - 2)
                    m_turn(2 * i - 1)
                    m_attend(2 * i - 2)
                    m_attend(2 * i - 1)
            for i in range(KT):
                project(("mo", i), ehi, elo, 0, L,
                        (lambda kt: pe.wait_ge(S("mo_split"), kt + 1)) if i == 0 else None)
            sums(6 * KT, META, T, 8)


MASKS = {}
MASK_COLS = 0
for _name, _n in (("identity", P), ("ones", L), ("neg_ones", P), ("neg_tri", P), ("stick", ZC), ("stick_neg", ZC),
                  ("causal", CC), ("causal_neg", CC), ("restart", L), ("chunk", L), ("eps", 1), ("one", 1)):
    MASKS[_name] = (MASK_COLS, _n)
    MASK_COLS += _n
ARENA = 16600


def mask_array():
    m = np.zeros((P, MASK_COLS), np.float32)

    def put(name, a):
        o, n = MASKS[name]
        m[:, o:o + n] = a

    r = np.arange(P)[:, None]
    put("identity", np.eye(P))
    put("ones", 1.0)
    put("neg_ones", -1.0)
    put("neg_tri", -(r >= np.arange(P)[None]).astype(np.float32))
    ok = np.concatenate([(k0 + r) < (t0 + np.arange(T - t0))[None] for c0, k0, t0 in SEG], 1)
    put("stick", ok)
    put("stick_neg", np.where(ok, 0.0, -30000.0))
    put("causal", np.concatenate([r <= np.arange(L)[None], r <= np.arange(P)[None]], 1))
    qk = np.concatenate([np.arange(P)[None] <= r, np.arange(L)[None] <= r + P], 1)
    put("causal_neg", np.where(qk, 0.0, -1e30))
    put("restart", (np.arange(L) % 64 != 0)[None])
    j, i = np.arange(P)[:, None], np.arange(P)[None]
    blk = ((j // 64 == i // 64) & (j <= i)).astype(np.float32)
    put("chunk", np.concatenate([blk, blk], 1))
    put("eps", EPS)
    put("one", 1.0)
    return m


def kernel(**inputs):
    import concourse.bacc as bacc
    from concourse.bass_utils import run_bass_kernel_spmd

    f = {k: np.asarray(v) for k, v in inputs.items()}
    mats = {k: f[k][0] for k in ("w_in", "w_proj_conv", "w_proj_attn", "w_out", "w_up_gate", "w_down", "even_w_in_2",
                                 "even_w_out_2", "odd_w_in_2", "odd_w_out_2")}
    small = np.zeros((D, P), np.float32)
    small[:, 0:16] = mats["even_w_in_2"][:, E_DT:E_DT + 16]
    small[:, LR_ROW:LR_ROW + 16] = mats["even_w_in_2"][:, E_LR:E_LR + 16]
    mats["small"] = small
    weights = np.empty((NCHUNKS, P, CW), np.float32)
    b = 0
    for _, _, blocks, _ in STREAM:
        for name, kt, col, width in blocks:
            weights[b // BPC, :, (b % BPC) * P:(b % BPC) * P + P] = mats[name][kt * P:kt * P + P, col:col + P]
            b += 1
    tokens = np.concatenate([f["meta_tokens"], f["x"][0]], 0)
    xT = np.ascontiguousarray(tokens.T.reshape(KT, P, T).transpose(1, 0, 2)).reshape(P, KT * T)
    prm = np.zeros((P, NPARAM), np.float32)

    def put(name, a):
        a = np.asarray(a).reshape(-1)
        n = a.size // P
        prm[:, PARAMS[name]:PARAMS[name] + n] = a.reshape(n, P).T

    for name, key in (("g_pre_mix",) * 2, ("g_post_mix",) * 2, ("g_pre_ffn",) * 2, ("g_post_ffn",) * 2,
                      ("even_norm", "even_norm_2"), ("ssd_norm", "even_ssd_norm_2"), ("odd_norm", "odd_norm_2"),
                      ("final_norm", "final_norm_2"), ("conv_mix", "conv_w_mix"), ("b_gate", "b_gate"),
                      ("conv_ffn", "conv_w_ffn"), ("even_conv", "even_conv_w_2"), ("even_conv_b", "even_conv_b_2"),
                      ("gate_b", "even_gate_b_2"), ("gla_norm", "even_gla_norm_2")):
        put(name, f[key])
    put("d_skip", np.repeat(f["even_d_skip_2"][0], 64))
    prm[0:16, PARAMS["dt_bias"]] = f["even_dt_bias_2"][0]
    prm[0:16, PARAMS["a_log"]] = f["even_a_log_2"][0]
    gw = np.zeros((P, 512), np.float32)
    gw[LR_ROW:LR_ROW + 16] = f["even_gate_w2_2"][0]

    nc = bacc.Bacc("TRN2", target_bir_lowering=False, num_devices=1)
    arrays = {"xT_in": xT, "params_in": prm, "weights_in": weights, "masks_in": mask_array(), "gate_w2_in": gw}
    aps = {k: nc.dram_tensor(k, a.shape, F32, kind="ExternalInput").ap() for k, a in arrays.items()}
    out = nc.dram_tensor("out", (P, KT, L), F32, kind="ExternalOutput").ap()
    scratch = nc.dram_tensor("decay_rows", (HEADS, L), F32).ap()
    build(nc, aps["xT_in"], aps["params_in"], aps["weights_in"], aps["masks_in"], aps["gate_w2_in"], out, scratch)
    r = run_bass_kernel_spmd(nc, [arrays], core_ids=[0])
    got = r.results[0]["out"]
    return np.ascontiguousarray(got.transpose(2, 1, 0)).reshape(1, L, D)
```

```python
from contextlib import ExitStack

import numpy as np
import concourse.bass as bass
from concourse import mybir

F32 = mybir.dt.float32
F32R = mybir.dt.float32r
I32 = mybir.dt.int32
ALU = mybir.AluOpType
ACT = mybir.ActivationFunctionType
AX_X = mybir.AxisListType.X

P = 128
D = 1024
KT = D // P
META = 16
L = 256
T = META + L
TA = META - 2
TC = TA - 2
NA = T - TA
FF = 2816
FT = FF // P
HEADS = 16
EPS = 1e-6

E_Z, E_XS, E_B, E_C, E_DT, E_Q, E_K, E_V, E_LR, E_G = 0, 1024, 2048, 2176, 2304, 2320, 2832, 3344, 4368, 4384
LR_ROW = 32

SEG = ((0, 0, TA), (NA, 128, 128), (NA + T - 128, 256, 256))
ZC = NA + (T - 128) + (T - 256)
CC = 256 + 128


MZ_LAG = 2


def tiles_of_stream():
    out = []

    def w(stage, i, name, col, k=KT, k0=0):
        out.append((stage, i, [(name, kt, col) for kt in range(k0, k0 + k)], 1))

    def x(stage, i, name, col, n):
        out.append((stage, i, [(name, kt, col + c * P) for kt in range(KT) for c in range(2)], n))

    for i in range(KT):
        w("k", i, "w_in", 4096 + i * P)
    for i in range(4):
        x("v", i, "w_in", 5120 + i * 256, 3)
    for i in range(KT):
        w("q", i, "w_in", 3072 + i * P)
        w("c", i, "w_in", 1024 + i * P)
        w("h", i, "w_in", 2048 + i * P)
        w("b", i, "w_in", i * P)
    for i in range(0, KT, 2):
        for j in (i, i + 1):
            w("gc", j, "w_in", 6144 + j * P)
            w("ga", j, "w_in", 7168 + j * P)
            w("pc", j, "w_proj_conv", j * P)
        for j in (i, i + 1):
            w("pa", j, "w_proj_attn", j * P)
    for i in range(KT):
        w("wo", i, "w_out", i * P)
    for i in range(FT):
        w("fu", i, "w_up_gate", i * P)
        w("fg", i, "w_up_gate", FF + i * P)
    for i in range(KT):
        w("fd", i, "w_down", i * P, FT)
    w("es", 0, "small", 0)
    w("eb", 0, "even_w_in_2", E_B)
    w("ec", 0, "even_w_in_2", E_C)
    for i in (0, 1):
        w("ex", i, "even_w_in_2", E_XS + i * P)
    for p in range(4):
        w("eq", p, "even_w_in_2", E_Q + p * P)
        w("ek", p, "even_w_in_2", E_K + p * P)
        x("ev", p, "even_w_in_2", E_V + p * 256, 2)
        for u in (2 * p, 2 * p + 1):
            w("ez", u, "even_w_in_2", E_Z + u * P)
            w("eg", u, "even_w_in_2", E_G + u * P)
            if u + 2 < KT:
                w("ex", u + 2, "even_w_in_2", E_XS + (u + 2) * P)
    for i in range(KT):
        w("eo1", i, "even_w_out_2", i * P)
    for i in range(KT):
        w("eo2", i, "even_w_out_2", i * P, k0=KT)
    for i in range(KT):
        w("mk", i, "odd_w_in_2", 1024 + i * P)
    for i in range(4):
        x("mv", i, "odd_w_in_2", 2048 + i * 256, 2)
    for i in range(KT + MZ_LAG):
        if i < KT:
            w("mq", i, "odd_w_in_2", i * P)
        if i >= MZ_LAG:
            w("mz", i - MZ_LAG, "odd_w_in_2", 3072 + (i - MZ_LAG) * P)
    for i in range(KT):
        w("mo", i, "odd_w_out_2", i * P)
    return out


BPC = 8
CW = BPC * P
STREAM = tiles_of_stream()
FIRST_BLOCK, FIRST_OUT = {}, {}
_b = _o = 0
for _s, _i, _blocks, _n in STREAM:
    FIRST_BLOCK[_s, _i], FIRST_OUT[_s, _i] = _b, _o
    _b += len(_blocks)
    _o += _n
NBLOCKS, NOUTS = _b, _o
NCHUNKS = NBLOCKS // BPC
assert NCHUNKS * BPC == NBLOCKS
BLOCKS_OF = {(s, i): len(b) for s, i, b, n in STREAM}
OUTS_OF = {(s, i): n for s, i, b, n in STREAM}

PARAMS = {}
NPARAM = 0
for _name, _n in (("g_pre_mix", 8), ("g_post_mix", 8), ("g_pre_ffn", 8), ("g_post_ffn", 8), ("even_norm", 8),
                  ("ssd_norm", 8), ("odd_norm", 8), ("final_norm", 8), ("conv_mix", 24), ("b_gate", 16),
                  ("conv_ffn", 3 * FT), ("even_conv", 40), ("even_conv_b", 10), ("d_skip", 8), ("gate_b", 4),
                  ("gla_norm", 1), ("dt_bias", 1), ("a_log", 1)):
    PARAMS[_name] = NPARAM
    NPARAM += _n

RAW = 4
RING = 4


def build(nc, xT, params, weights, masks, gate_w2, out, scratch):
    with ExitStack() as ctx:
        def sb(name, cols, dt=F32):
            return ctx.enter_context(nc.sbuf_tensor(name, [P, cols], dt))

        sems = {}

        def S(name):
            if name not in sems:
                sems[name] = ctx.enter_context(nc.semaphore(name))
            return sems[name]

        raw = sb("raw_weights", RAW * CW)
        whi = sb("weights_hi", RING * CW, F32R)
        wlo = sb("weights_lo", RING * CW, F32R)
        xhi_t = sb("x_hi", KT * T, F32R)
        xlo_t = sb("x_lo", KT * T, F32R)
        YW = 3 * KT * NA
        yhi_t = sb("y_hi", YW, F32R)
        ylo_t = sb("y_lo", YW, F32R)
        h_t = sb("hidden", KT * T)
        prm = sb("params", NPARAM)
        msk = sb("masks", MASK_COLS)
        gw2 = sb("gate_w2", 512)
        rinv = sb("rinv", T)
        rpost = sb("rinv_post", T)
        rcol = sb("rinv_by_token", 4)
        arena = sb("arena", ARENA)
        acol = sb("decay_rate", 2)
        scans = sb("dt_and_cumsum", 256)

        ps = ctx.enter_context(nc.psum_tensor("ps", [P, 8, 512], F32))

        def v3(ap, n):
            return ap.rearrange("p (a b) -> p a b", a=n)

        xhi, xlo, H = v3(xhi_t[:], KT), v3(xlo_t[:], KT), v3(h_t[:], KT)
        yhi = yhi_t[:].rearrange("p (s a b) -> p s a b", s=3, a=KT)
        ylo = ylo_t[:].rearrange("p (s a b) -> p s a b", s=3, a=KT)
        fhi, flo = v3(yhi_t[:, 0:FT * L], FT), v3(ylo_t[:, 0:FT * L], FT)
        ehi, elo = v3(yhi_t[:, 0:16 * L], 16), v3(ylo_t[:, 0:16 * L], 16)
        CONV, ATT, MERGED = 0, 1, 2

        def mask(name):
            o, n = MASKS[name]
            return msk[:, o:o + n]

        def pcol(name, i=0):
            c = PARAMS[name] + i
            return prm[:, c:c + 1]

        class Area:
            def __init__(self, at=0):
                self.at = at

            def __call__(self, *shape):
                n = int(np.prod(shape))
                ap = arena[:, self.at:self.at + n]
                self.at += n
                assert self.at <= ARENA, self.at
                if len(shape) == 2:
                    ap = ap.rearrange("p (a b) -> p a b", a=shape[0])
                if len(shape) == 3:
                    ap = ap.rearrange("p (a b c) -> p a b c", a=shape[0], b=shape[1])
                return ap

        A1 = Area()
        keysT = A1(KT, 3 * P)
        vals = A1(3, D)
        qpair = A1(2, 2, T)
        sp = A1(2, ZC)
        fz = A1(2, ZC)
        aw = A1(2, ZC)
        cbuf = A1(2, T)
        chbuf = A1(2, T)
        cv = A1(2, NA)
        bb = A1(2, NA)
        gate = A1(4, NA)
        mm1 = A1(2, NA)
        A2 = Area()
        mout = A2(KT, T)
        A3 = Area(ARENA - KT * T)
        sq = A3(KT, T)
        assert A1.at <= ARENA - KT * T
        A4 = Area(KT * T)
        fu = A4(2, NA)
        fcv = A4(2, L)
        fgl = A4(2, L)
        fy = A4(2, L)
        A5 = Area()
        xs = A5(KT, L)
        gcs = A5(4, L)
        cb = A5(2, CC)
        tkc = A5(2, P)
        e_q = A5(2, L)
        e_k = A5(2, L)
        vb = A5(2, 2, L)
        th = A5(2, L)
        zs = A5(2, L)
        gs = A5(4, L)
        xd = A5(2, P)
        dec = A5(2, CC)
        bc = A5(2, 2, L)
        sqy = A5(2, L)
        scr2 = A5(2, L + 4)
        A7 = Area(A5.at)
        bT = A7(L)
        cT = A7(2, L)
        sm = A7(L)
        small1 = A7(L)
        small2 = A7(L)
        acs = A7(L)
        gtmp = A7(2, L)
        cvo = A7(L)
        A10 = Area(A5.at)
        ka = A10(2, L)
        kb = A10(2, L)
        eg = A10(2, L)
        em = A10(L)
        qe = A10(2, 2, L)
        qg = A10(2, 2, L)
        klt = A10(2, 2, P)
        st = A10(3, P)
        sc = A10(2, L)
        osq = A10(512)
        orv = A10(512)
        A9 = Area()
        mkT = A9(KT, L)
        mval = A9(2, D)
        mqp = A9(2, 2, L)
        mzs = A9(4, L)
        mz = A9(2, L)
        pr = A9(4, CC)
        prT = A9(2, CC)
        mst = A9(4, 8)
        mo = A9(2, L)

        SSB = 7

        def bank(n):
            return ps[:, n, :]

        block = ctx.enter_context(nc.Block())

        class Steps:
            def __init__(self, eng, own):
                self.eng, self.own, self.n, self.last = eng, own, {}, None

            def sig(self, ins, name, k=1):
                ins.then_inc(S(name), k)
                self.n[name] = self.n.get(name, 0) + k
                self.last = (name, self.n[name])
                return ins

            def step(self, ins):
                return self.sig(ins, self.own)

            def settle(self):
                if self.last:
                    self.eng.wait_ge(S(self.last[0]), self.last[1])

        def need(eng, name, n):
            if n > 0:
                eng.wait_ge(S(name), n)

        freed = {}
        parts = 0
        for s_, i_, b_, n_ in STREAM:
            f = FIRST_BLOCK[s_, i_]
            for j in range(len(b_)):
                if (f + j) % BPC == BPC - 1:
                    if j == len(b_) - 1:
                        freed[(f + j) // BPC] = ("out_ready", FIRST_OUT[s_, i_] + n_)
                    elif n_ > 1:
                        parts += 1
                        freed[(f + j) // BPC] = ("chunk_read", parts)
                    else:
                        parts += 1
                        freed[(f + j) // BPC] = ("chunk_read", parts)

        def chunk_of(tile):
            f = FIRST_BLOCK[tile]
            return [c for c in range(f // BPC, (f + BLOCKS_OF[tile]) // BPC + 1)
                    if f <= c * BPC + BPC - 1 < f + BLOCKS_OF[tile]]

        taken = {}
        cnt = {}
        for s_, i_, b_, n_ in STREAM:
            name = {"gc": "gate_raw", "ga": "gate_raw", "pc": "conv_merged", "pa": "att_merged", "wo": "mout_ready",
                    "fd": "mout_ready", "fu": "u_ready", "fg": "ffn_y", "es": "small_ready", "ez": "z_half",
                    "eg": "z_half", "eo1": "eo1_taken", "eo2": "h_ready", "mo": "h_ready", "mz": "mz_half"}.get(s_, "out_taken")
            for o in range(n_):
                if name == "h_ready" and s_ == "eo2" and i_ == 0:
                    cnt[name] = 2 * KT
                cnt[name] = cnt.get(name, 0) + 1
                taken[FIRST_OUT[s_, i_] + o] = (name, cnt[name])

        HALF = {t: n for n, t in enumerate((s_, i_) for s_, i_, b_, n_ in STREAM if s_ in ("eb", "ec", "ex", "ez", "eg"))}
        CONVS = [t for t in HALF if t[0] in ("eb", "ec", "ex")]
        K_TAKEN = [taken[FIRST_OUT["ek", p]][1] for p in range(4)]

        @block.sync
        def _(sp_):
            half = KT // 2 * T
            for c in range(NCHUNKS):
                if c < 2:
                    sp_.dma_start(h_t[:, c * half:(c + 1) * half], xT[:, c * half:(c + 1) * half]).then_inc(
                        S(f"load_x{c}"), 16)
                if c >= RAW:
                    sp_.wait_ge(S("lo_ready"), c - RAW + 1)
                s = c % RAW
                sp_.dma_start(raw[:, s * CW:(s + 1) * CW], weights[c]).then_inc(S(f"raw{s}"), 16)

        @block.gpsimd
        def _(pool):
            g = Steps(pool, "pool_step")
            g.sig(nc.gpsimd.memset(keysT[:, :, T:3 * P], 0.0), "zeroed")
            g.sig(nc.gpsimd.memset(vals[:, 2, :], 0.0), "zeroed")
            g.sig(nc.gpsimd.memset(qpair, 0.0), "zeroed")
            def add_normed(first, t0):
                for kt in range(KT):
                    pool.wait_ge(S("normed"), first + kt + 1)
                    g.settle()
                    g.sig(nc.gpsimd.tensor_tensor(H[:, kt, t0:T], H[:, kt, t0:T], mout[:, kt, t0:T], ALU.add),
                          "h_ready")

            add_normed(0, TA)
            for i in range(FT):
                pool.wait_ge(S("gelu_ready"), i + 1)
                g.settle()
                g.sig(nc.gpsimd.tensor_tensor(fgl[:, i % 2, :], fgl[:, i % 2, :], rinv[:, META:T], ALU.mult),
                      "gelu_scaled")
                pool.wait_ge(S("ffn_hi"), i + 1)
                g.settle()
                g.sig(nc.gpsimd.tensor_tensor(flo[:, i, :], fy[:, i % 2, :], fhi[:, i, :].bitcast(F32),
                                              ALU.subtract), "ffn_split")
            add_normed(KT, META)
            pool.wait_ge(S("rms_ready"), 5)
            g.sig(nc.gpsimd.memset(cT, 0.0), "zeroed")
            g.sig(nc.gpsimd.memset(scr2[:, :, 0:3], 0.0), "zeroed")
            g.sig(nc.gpsimd.memset(scans[:], 0.0), "zeroed")
            pool.wait_ge(S("cb_taken"), 2)
            pool.wait_ge(S("xsilu"), 2)
            pool.wait_ge(S("bc_out"), 16)
            for buf in (qe, qg, sc):
                g.sig(nc.gpsimd.memset(buf, 0.0), "zeroed")

            def ssd_weights(u):
                for h in (2 * u, 2 * u + 1):
                    pool.wait_ge(S("decay_exp"), h + 1)
                    g.settle()
                    g.sig(nc.gpsimd.tensor_tensor(dec[:, h % 2, :], dec[:, h % 2, :], cb[:, h // 8, :], ALU.mult),
                          "m_ready")

            def gla_products(p):
                k = p % 2
                pool.wait_ge(S("gla_exp"), p + 1)
                pool.wait_ge(S("out_taken"), K_TAKEN[p])
                need(pool, "gla_o", p - 1)
                g.settle()
                g.sig(nc.gpsimd.tensor_tensor(kb[:, k, :], kb[:, k, :], e_k[:, k, :], ALU.mult), "gla_kl")
                g.settle()
                g.step(nc.gpsimd.tensor_tensor(ka[:, k, :], ka[:, k, :], e_k[:, k, :], ALU.mult))
                for e in range(2):
                    rows = slice(64 * e, 64 * e + 64)
                    g.settle()
                    g.step(nc.gpsimd.tensor_tensor(qg[rows, k, e, :], eg[rows, k, :], e_q[rows, k, :], ALU.mult))
                    g.settle()
                    ins = nc.gpsimd.tensor_tensor(qe[rows, k, e, :], em[rows], e_q[rows, k, :], ALU.mult)
                    g.sig(ins, "gla_qk") if e else g.step(ins)

            for p in range(4):
                ssd_weights(2 * p)
                gla_products(p)
                ssd_weights(2 * p + 1)
            pool.wait_ge(S("h_ready"), 3 * KT)
            g.sig(nc.gpsimd.memset(mqp, 0.0), "zeroed")

        @block.scalar
        def _(act):
            a = Steps(act, "act_step")
            A = nc.scalar.activation

            def exp_and_ln():
                nc.scalar.preload_act_table_set("natural_log_exp_and_others")

            exp_and_ln()
            act.dma_start(prm[:], params).then_inc(S("load_params"), 16)
            nxt = [0]

            def split_hi():
                c = nxt[0]
                nxt[0] += 1
                if c >= NCHUNKS:
                    return
                act.wait_ge(S(f"raw{c % RAW}"), 16 * (c // RAW + 1))
                if c >= RING:
                    act.wait_ge(S(freed[c - RING][0]), freed[c - RING][1])
                    act.wait_ge(S("lo_ready"), c - RING + 1)
                s = c % RING
                a.sig(A(whi[:, s * CW:(s + 1) * CW], raw[:, (c % RAW) * CW:(c % RAW + 1) * CW], ACT.Copy), "hi_ready")

            def feed(tile):
                for _ in chunk_of(tile):
                    split_hi()

            def x_high(n, gain, t0, base):
                for kt in range(KT):
                    if base is not None:
                        act.wait_ge(S("h_ready"), base + kt + 1)
                    elif kt == KT // 2:
                        act.wait_ge(S("load_x1"), 16)
                    a.sig(A(xhi[:, kt, t0:T], H[:, kt, t0:T], ACT.Copy, scale=pcol(gain, kt)), "x_hi")
                    a.sig(A(sq[:, kt, t0:T], H[:, kt, t0:T], ACT.Square), "sq_ready")

            def inverse_rms(dst, width, total, nth, src=None, cols=None):
                act.wait_ge(S("sums_ready"), nth)
                src = bank(SSB)[:, 0:width] if src is None else src
                a.step(A(dst, src, ACT.Ln, scale=1.0 / total, bias=epsb))
                a.settle()
                a.sig(A(dst, dst, ACT.Exp, scale=-0.5), "rms_ready")

            epsb = mask("eps")
            one = mask("one")
            act.wait_ge(S("load_params"), 16)
            act.wait_ge(S("load_x0"), 16)
            act.dma_start(msk[:], masks).then_inc(S("load_masks"), 16)
            act.dma_start(gw2[:], gate_w2).then_inc(S("load_gate"), 16)
            split_hi()
            x_high(0, "g_pre_mix", 0, None)
            for _ in range(RING - 1):
                split_hi()
            act.wait_ge(S("load_masks"), 16)
            inverse_rms(rinv[:, 0:T], T, D, 1)
            for i in range(KT):
                feed(("k", i))
            for i in range(4):
                feed(("v", i))

            def softplus_part(h):
                act.wait_ge(S("z_ready"), h + 1)
                need(act, "f_ready", h - 1)
                a.settle()
                a.step(A(sp[:, h % 2, :], bank(4 + h % 2)[:, 0:ZC], ACT.Abs))
                a.settle()
                a.step(A(sp[:, h % 2, :], sp[:, h % 2, :], ACT.Exp, scale=-1.0))
                a.settle()
                a.sig(A(sp[:, h % 2, :], sp[:, h % 2, :], ACT.Ln, bias=one), "sp_ready")

            def weights_of(h):
                act.wait_ge(S("loga_taken"), h + 1)
                need(act, "av_ready", h - 1)
                a.sig(A(aw[:, h % 2, :], fz[:, h % 2, :], ACT.Exp), "a_ready")

            def att_high(p):
                act.wait_ge(S("av_ready"), 2 * p + 2)
                a.sig(A(yhi[:, ATT, p, :], bank(6 + p % 2)[:, 0:NA], ACT.Copy), "att_hi")

            for p in range(KT):
                if p >= 3:
                    att_high(p - 3)
                feed(("q", p))
                if p >= 2:
                    weights_of(2 * p - 3)
                if p:
                    softplus_part(2 * p - 2)
                feed(("c", p))
                feed(("h", p))
                if p:
                    weights_of(2 * p - 2)
                    softplus_part(2 * p - 1)
                feed(("b", p))
                act.wait_ge(S("conv_y"), p + 1)
                a.sig(A(yhi[:, CONV, p, :], bb[:, p % 2, :], ACT.Copy), "conv_hi")
            att_high(KT - 3)
            weights_of(13)
            softplus_part(14)
            feed(("gc", 0))
            weights_of(14)
            softplus_part(15)
            att_high(KT - 2)
            feed(("ga", 0))
            feed(("pc", 0))
            weights_of(15)
            feed(("gc", 1))
            att_high(KT - 1)
            for i in range(0, KT, 2):
                for j in (i, i + 1):
                    for k, s_ in enumerate(("gc", "ga")):
                        if (s_, j) not in (("gc", 0), ("ga", 0), ("gc", 1)):
                            feed((s_, j))
                        act.wait_ge(S("gate_raw"), 2 * j + k + 1)
                        g_ = gate[:, (2 * j + k) % 4, :]
                        a.sig(A(g_, g_, ACT.Sigmoid, bias=pcol("b_gate", KT * k + j)), "gate_ready")
                    if j:
                        feed(("pc", j))
                for j in (i, i + 1):
                    feed(("pa", j))
                    act.wait_ge(S("merged_y"), j + 1)
                    a.sig(A(yhi[:, MERGED, j, :], mm1[:, j % 2, :], ACT.Copy), "merged_hi")

            def out_squares(stage, n0, t0):
                for i in range(KT):
                    feed((stage, i))
                    act.wait_ge(S("mout_ready"), n0 + i + 1)
                    a.sig(A(sq[:, i, t0:T], mout[:, i, t0:T], ACT.Square), "sq_ready")

            out_squares("wo", 0, TA)
            exp_and_ln()
            inverse_rms(rpost[:, TA:T], NA, D, 2)
            x_high(1, "g_pre_ffn", TA, 0)
            inverse_rms(rinv[:, TA:T], NA, D, 3)
            for i in range(FT):
                feed(("fu", i))
                act.wait_ge(S("u_ready"), i + 1)
                a.sig(A(fcv[:, i % 2, :], fu[:, i % 2, 0:L], ACT.Copy, scale=pcol("conv_ffn", i)), "tap_ready")
                feed(("fg", i))
                act.wait_ge(S("u_conv"), i + 1)
                need(act, "ffn_y", i - 1)
                a.sig(A(fgl[:, i % 2, :], fcv[:, i % 2, :], ACT.Gelu_apprx_tanh), "gelu_ready")
                act.wait_ge(S("ffn_y"), i + 1)
                a.sig(A(fhi[:, i, :], fy[:, i % 2, :], ACT.Copy), "ffn_hi")
            out_squares("fd", KT, META)
            exp_and_ln()
            inverse_rms(rpost[:, META:T], L, D, 4)
            x_high(2, "even_norm", META, KT)
            inverse_rms(rinv[:, META:T], L, D, 5)

            feed(("es", 0))
            act.wait_ge(S("small_ready"), 1)
            a.step(A(small1[0:16, :], sm[0:16, :], ACT.Abs, bias=pcol("dt_bias")[0:16]))
            a.step(A(acol[0:16, 0:1], pcol("a_log")[0:16], ACT.Exp))
            a.settle()
            a.step(A(small1[0:16, :], small1[0:16, :], ACT.Exp, scale=-1.0))
            a.settle()
            a.sig(A(small1[0:16, :], small1[0:16, :], ACT.Ln, bias=one[0:16]), "dt_ln")

            def gate_log(i):
                act.wait_ge(S("lowrank"), i + 1)
                need(act, "decay_sum", i - 1)
                a.settle()
                b_ = bank(4 + i % 2)[:, 0:L]
                a.step(A(gtmp[:, i % 2, :], b_, ACT.Abs, bias=pcol("gate_b", i)))
                a.settle()
                a.step(A(gtmp[:, i % 2, :], gtmp[:, i % 2, :], ACT.Exp, scale=-1.0))
                a.settle()
                a.sig(A(gtmp[:, i % 2, :], gtmp[:, i % 2, :], ACT.Ln, bias=one), "gate_ln")

            feed(("eb", 0))
            gate_log(0)
            gate_log(1)
            feed(("ec", 0))
            gate_log(2)
            gate_log(3)
            act.wait_ge(S("acs_ready"), 1)
            act.dma_start(scratch, acs[0:16, :]).then_inc(S("bc_out"), 16)

            def spread(u):
                act.dma_start(bc[:, u % 2], scratch[2 * u:2 * u + 2, :].rearrange("(o h) t -> o h t", o=1)
                              .partition_broadcast(P)).then_inc(S(f"spread{u % 2}"), 16)

            def half_tanh(tile, src):
                if tile in CONVS:
                    act.wait_ge(S("xconv"), CONVS.index(tile) + 1)
                else:
                    act.wait_ge(S("z_half"), taken[FIRST_OUT[tile]][1])
                a.sig(A(th[:, HALF[tile] % 2, :], src, ACT.Tanh), "z_tanh")

            half_tanh(("eb", 0), bT)
            half_tanh(("ec", 0), cvo)
            for i in (0, 1):
                feed(("ex", i))
                half_tanh(("ex", i), xs[:, i, :])
            act.wait_ge(S("bc_out"), 16)
            spread(0)
            spread(1)

            def decay_exps(u):
                for h in (2 * u, 2 * u + 1):
                    act.wait_ge(S("decay_arg"), h + 1)
                    a.sig(A(dec[:, h % 2, :], dec[:, h % 2, :], ACT.Exp), "decay_exp")
                if u + 2 < KT:
                    spread(u + 2)

            def ssd_high(u):
                act.wait_ge(S("yz_ready"), u + 1)
                need(act, "sum_part", u - 1)
                a.sig(A(ehi[:, u, :], xs[:, u, :], ACT.Copy, scale=pcol("ssd_norm", u)), "ye_hi")
                a.sig(A(sqy[:, u % 2, :], xs[:, u, :], ACT.Square), "sqy_ready")

            def gla_exps(p):
                k = p % 2
                act.wait_ge(S("gla_arg"), p + 1)
                need(act, "gla_qk", p)
                need(act, "st_ready", p - 1)
                a.step(A(em, ka[:, k, :], ACT.Exp, scale=1.0 / 16))
                a.step(A(kb[:, k, :], kb[:, k, :], ACT.Exp, scale=1.0 / 16))
                a.settle()
                a.step(A(ka[:, k, :], ka[:, k, :], ACT.Exp, scale=-1.0 / 16))
                a.sig(A(eg[:, k, :], gcs[:, p, :], ACT.Exp, scale=1.0 / 16), "gla_exp")

            def gla_squares(p):
                act.wait_ge(S("gla_o"), p + 1)
                a.sig(A(osq, bank(6), ACT.Square), "gla_sq")

            def gla_rms(p):
                act.wait_ge(S("gla_sums"), p + 1)
                need(act, "gla_og", 2 * p)
                a.settle()
                a.step(A(orv, bank(4), ACT.Ln, scale=1.0 / P, bias=epsb))
                a.settle()
                a.sig(A(orv, orv, ACT.Exp, scale=-0.5), "gla_rms")

            def gla_high(p):
                for h in (2 * p, 2 * p + 1):
                    act.wait_ge(S("gla_og"), h + 1)
                    a.sig(A(ehi[:, KT + h, :], gs[:, h % 4, :], ACT.Copy), "go_hi")

            for p in range(4):
                u = 2 * p
                feed(("eq", p))
                decay_exps(u)
                feed(("ek", p))
                if p:
                    gla_squares(p - 1)
                gla_exps(p)
                feed(("ev", p))
                if p:
                    gla_rms(p - 1)
                feed(("ez", u))
                half_tanh(("ez", u), zs[:, 0, :])
                decay_exps(u + 1)
                feed(("eg", u))
                half_tanh(("eg", u), gs[:, u % 4, :])
                if p:
                    gla_high(p - 1)
                ssd_high(u)
                if p < 3:
                    feed(("ex", u + 2))
                    half_tanh(("ex", u + 2), xs[:, u + 2, :])
                feed(("ez", u + 1))
                half_tanh(("ez", u + 1), zs[:, 1, :])
                feed(("eg", u + 1))
                half_tanh(("eg", u + 1), gs[:, (u + 1) % 4, :])
                ssd_high(u + 1)
                if p < 3:
                    feed(("ex", u + 3))
                    half_tanh(("ex", u + 3), xs[:, u + 3, :])
            gla_squares(3)
            exp_and_ln()
            feed(("eo1", 0))
            inverse_rms(rpost[:, 0:L], L, D, 6)
            gla_rms(3)
            gla_high(3)
            for i in range(1, KT):
                feed(("eo1", i))
            for i in range(KT):
                feed(("eo2", i))
            x_high(3, "odd_norm", META, 2 * KT)
            inverse_rms(rinv[:, META:T], L, D, 7)
            for i in range(KT):
                feed(("mk", i))
            for i in range(4):
                feed(("mv", i))

            def soft_exp(h):
                act.wait_ge(S("m_max"), h + 1)
                q, s_ = h % 4, mst[:, h % 4, :]
                a.step(A(pr[:, q, 0:P], pr[:, q, 0:P], ACT.Exp, bias=s_[:, 0:1], accum_out=s_[:, 2:3]))
                a.sig(A(pr[:, q, P:CC], pr[:, q, P:CC], ACT.Exp, bias=s_[:, 1:2], accum_out=s_[:, 3:4]), "m_exp")

            def prob_copy(h):
                act.wait_ge(S("p_T"), h + 1)
                a.sig(A(prT[:, h % 2, :], bank(5 + h % 2)[:, 0:CC], ACT.Copy), "p_taken")

            def m_high(j):
                act.wait_ge(S("mo_ready"), j + 1)
                a.sig(A(ehi[:, j, :], mo[:, j % 2, :], ACT.Copy), "mo_hi")

            for i in range(KT + 3):
                if i < KT:
                    feed(("mq", i))
                if 2 <= i <= KT + 1:
                    prob_copy(2 * i - 4)
                if 1 <= i <= KT:
                    soft_exp(2 * i - 2)
                j = i - MZ_LAG
                if 0 <= j < KT:
                    feed(("mz", j))
                    act.wait_ge(S("mz_half"), j + 1)
                    a.sig(A(mzs[:, j % 4, :], mz[:, j % 2, :], ACT.Tanh), "mz_tanh")
                if 2 <= i <= KT + 1:
                    prob_copy(2 * i - 3)
                if 1 <= i <= KT:
                    soft_exp(2 * i - 1)
                if i >= 3:
                    m_high(i - 3)
            for i in range(KT):
                feed(("mo", i))
                act.wait_ge(S("h_ready"), 3 * KT + i + 1)
                a.sig(A(sq[:, i, META:T], H[:, i, META:T], ACT.Square), "sq_ready")
            exp_and_ln()
            inverse_rms(rinv[:, META:T], L, D, 8)
            for i in range(KT):
                act.wait_ge(S("final"), i + 1)
                act.dma_start(out[:, i, :], mout[:, i, 0:L]).then_inc(S("stored"), 16)
            act.wait_ge(S("stored"), 16 * KT)

        @block.vector
        def _(dve):
            d = Steps(dve, "dve_step")
            V = nc.vector
            nxt = [0]
            TT, STT, TS = V.tensor_tensor, V.scalar_tensor_tensor, V.tensor_scalar

            def split_lo():
                c = nxt[0]
                nxt[0] += 1
                if c >= NCHUNKS:
                    return
                dve.wait_ge(S("hi_ready"), c + 1)
                s = c % RING
                d.sig(TT(wlo[:, s * CW:(s + 1) * CW], raw[:, (c % RAW) * CW:(c % RAW + 1) * CW],
                         whi[:, s * CW:(s + 1) * CW].bitcast(F32), ALU.subtract), "lo_ready")

            def feed(tile):
                for _ in chunk_of(tile):
                    split_lo()

            def result(tile, o=0, width=NA):
                n = FIRST_OUT[tile] + o
                dve.wait_ge(S("out_ready"), n + 1)
                return bank(n % 4)[:, 0:width]

            def x_low(gain, t0, base):
                for kt in range(KT):
                    dve.wait_ge(S("x_hi"), base + kt + 1)
                    d.sig(STT(out=xlo[:, kt, t0:T], in0=H[:, kt, t0:T], scalar=pcol(gain, kt),
                              in1=xhi[:, kt, t0:T].bitcast(F32), op0=ALU.mult, op1=ALU.subtract), "x_split")

            dve.wait_ge(S("load_params"), 16)
            split_lo()
            x_low("g_pre_mix", 0, 0)
            for _ in range(RING - 1):
                split_lo()
            dve.wait_ge(S("load_masks"), 16)
            dve.wait_ge(S("rms_ready"), 1)
            for i in range(KT):
                r = result(("k", i), 0, T)
                d.sig(TT(keysT[:, i, 0:T], r, rinv[:, 0:T], ALU.mult), "out_taken")
                feed(("k", i))
            dve.wait_ge(S("rinv_T"), 1)
            d.step(V.tensor_copy(rcol[:, 0:1], bank(6)[:, 0:1]))
            d.step(V.tensor_copy(rcol[:, 1:2], bank(6)[:, P:P + 1]))
            d.step(V.tensor_copy(rcol[0:T - L, 2:3], bank(6)[0:T - L, 2 * P:2 * P + 1]))
            d.settle()
            dve.wait_ge(S("zeroed"), 3)
            for i in range(4):
                for o in range(3):
                    n = P if o < 2 else T - L
                    r = result(("v", i), o, L)
                    d.sig(TS(vals[0:n, o, 256 * i:256 * i + 256], r[0:n], rcol[0:n, o:o + 1], None, ALU.mult),
                          "out_taken")
                feed(("v", i))

            def fail(h):
                dve.wait_ge(S("sp_ready"), h + 1)
                need(dve, "a_ready", h - 1)
                d.settle()
                d.step(STT(out=fz[:, h % 2, :], in0=bank(4 + h % 2)[:, 0:ZC], scalar=0.0, in1=sp[:, h % 2, :],
                           op0=ALU.max, op1=ALU.add))
                d.settle()
                d.sig(TT(fz[:, h % 2, :], fz[:, h % 2, :], mask("stick"), ALU.mult), "f_ready")

            def log_weight(h):
                dve.wait_ge(S("loga_ready"), h + 1)
                d.settle()
                d.sig(STT(out=fz[:, h % 2, :], in0=bank(4 + h % 2)[:, 0:ZC], scalar=0.0, in1=mask("stick_neg"),
                          op0=ALU.min, op1=ALU.add), "loga_taken")

            def att_low(p):
                dve.wait_ge(S("att_hi"), p + 1)
                d.sig(TT(ylo[:, ATT, p, :], bank(6 + p % 2)[:, 0:NA], yhi[:, ATT, p, :].bitcast(F32), ALU.subtract),
                      "att_split")

            def conv_low(p):
                dve.wait_ge(S("conv_hi"), p + 1)
                d.sig(TT(ylo[:, CONV, p, :], bb[:, p % 2, :], yhi[:, CONV, p, :].bitcast(F32), ALU.subtract),
                      "conv_split")

            for p in range(KT):
                if p >= 3:
                    att_low(p - 3)
                r = result(("q", p), 0, NA)
                need(dve, "z_ready", 2 * p - 2)
                for e in range(2):
                    rows = slice(64 * e, 64 * e + 64)
                    ins = STT(out=qpair[rows, p % 2, e, TA:T], in0=r[rows], scalar=0.125, in1=rinv[rows, TA:T],
                              op0=ALU.mult, op1=ALU.mult)
                    d.sig(ins, "out_taken") if e else d.step(ins)
                if p >= 2:
                    log_weight(2 * p - 3)
                feed(("q", p))
                r = result(("c", p), 0, T - TC)
                d.settle()
                d.sig(TT(cbuf[:, p % 2, TC:T], r, rinv[:, TC:T], ALU.mult), "out_taken")
                if p:
                    fail(2 * p - 2)
                feed(("c", p))
                r = result(("h", p), 0, T - TC)
                ch = chbuf[:, p % 2, :]
                d.settle()
                d.sig(TT(ch[:, TC:T], r, rinv[:, TC:T], ALU.mult), "out_taken")
                feed(("h", p))
                d.settle()
                d.step(TT(ch[:, TC:T], ch[:, TC:T], cbuf[:, p % 2, TC:T], ALU.mult))
                if p:
                    log_weight(2 * p - 2)
                d.settle()
                c_ = cv[:, p % 2, :]
                d.step(TS(c_, ch[:, TC:T - 2], pcol("conv_mix", p), None, ALU.mult))
                for j in (1, 2):
                    d.settle()
                    d.step(STT(out=c_, in0=ch[:, TC + j:T - 2 + j], scalar=pcol("conv_mix", KT * j + p), in1=c_,
                               op0=ALU.mult, op1=ALU.add))
                if p:
                    conv_low(p - 1)
                    fail(2 * p - 1)
                r = result(("b", p), 0, NA)
                d.settle()
                d.sig(TT(bb[:, p % 2, :], r, rinv[:, TA:T], ALU.mult), "out_taken")
                feed(("b", p))
                d.settle()
                d.sig(TT(bb[:, p % 2, :], bb[:, p % 2, :], c_, ALU.mult), "conv_y")
            conv_low(KT - 1)

            def gate_raw(s, i, j):
                r = result((s, i), 0, NA)
                d.settle()
                d.sig(TT(gate[:, (2 * i + j) % 4, :], r, rinv[:, TA:T], ALU.mult), "gate_raw")
                feed((s, i))

            def conv_branch(i):
                r = result(("pc", i), 0, NA)
                dve.wait_ge(S("gate_ready"), 2 * i + 1)
                d.settle()
                d.sig(TT(mm1[:, i % 2, :], r, gate[:, (2 * i) % 4, :], ALU.mult), "conv_merged")
                feed(("pc", i))

            att_low(KT - 3)
            log_weight(13)
            fail(14)
            gate_raw("gc", 0, 0)
            log_weight(14)
            fail(15)
            att_low(KT - 2)
            gate_raw("ga", 0, 1)
            log_weight(15)
            for i in range(0, KT, 2):
                for j in (i, i + 1):
                    if j:
                        gate_raw("gc", j, 0)
                        if j == 1:
                            att_low(KT - 1)
                            conv_branch(0)
                        gate_raw("ga", j, 1)
                        conv_branch(j)
                for j in (i, i + 1):
                    r = result(("pa", j), 0, NA)
                    dve.wait_ge(S("gate_ready"), 2 * j + 2)
                    g2 = gate[:, (2 * j + 1) % 4, :]
                    d.settle()
                    d.sig(TT(g2, r, g2, ALU.mult), "att_merged")
                    feed(("pa", j))
                    d.settle()
                    d.sig(TT(mm1[:, j % 2, :], mm1[:, j % 2, :], g2, ALU.add), "merged_y")
                for j in (i, i + 1):
                    dve.wait_ge(S("merged_hi"), j + 1)
                    d.sig(TT(ylo[:, MERGED, j, :], mm1[:, j % 2, :], yhi[:, MERGED, j, :].bitcast(F32), ALU.subtract),
                          "merged_split")

            def out_tiles(stage, t0):
                for i in range(KT):
                    r = result((stage, i), 0, T - t0)
                    d.sig(V.tensor_copy(mout[:, i, t0:T], r), "mout_ready")
                    feed((stage, i))

            def post_norm(nth, gain_post, gain_pre, base, t0):
                dve.wait_ge(S("rms_ready"), nth)
                d.settle()

                def low(kt):
                    dve.wait_ge(S("x_hi"), base + kt + 1)
                    d.sig(STT(out=xlo[:, kt, t0:T], in0=H[:, kt, t0:T], scalar=pcol(gain_pre, kt),
                              in1=xhi[:, kt, t0:T].bitcast(F32), op0=ALU.mult, op1=ALU.subtract), "x_split")

                for kt in range(KT):
                    m = mout[:, kt, t0:T]
                    d.sig(STT(out=m, in0=m, scalar=pcol(gain_post, kt), in1=rpost[:, t0:T], op0=ALU.mult, op1=ALU.mult),
                          "normed")
                    if kt >= 2:
                        low(kt - 2)
                low(KT - 2)
                low(KT - 1)

            out_tiles("wo", TA)
            post_norm(2, "g_post_mix", "g_pre_ffn", KT, TA)
            dve.wait_ge(S("rms_ready"), 3)
            for i in range(FT):
                u, c_ = fu[:, i % 2, :], fcv[:, i % 2, :]
                r = result(("fu", i), 0, NA)
                need(dve, "tap_ready", i - 1)
                d.settle()
                d.sig(TT(u, r, rinv[:, TA:T], ALU.mult), "u_ready")
                feed(("fu", i))
                dve.wait_ge(S("tap_ready"), i + 1)
                for j in (1, 2):
                    d.settle()
                    ins = STT(out=c_, in0=u[:, j:L + j], scalar=pcol("conv_ffn", FT * j + i), in1=c_,
                              op0=ALU.mult, op1=ALU.add)
                    d.sig(ins, "u_conv") if j == 2 else d.step(ins)
                r = result(("fg", i), 0, L)
                dve.wait_ge(S("gelu_scaled"), i + 1)
                need(dve, "ffn_split", i - 1)
                d.sig(TT(fy[:, i % 2, :], r, fgl[:, i % 2, :], ALU.mult), "ffn_y")
                feed(("fg", i))
            out_tiles("fd", META)
            post_norm(4, "g_post_ffn", "even_norm", 2 * KT, META)
            dve.wait_ge(S("rms_ready"), 5)
            rL = rinv[:, META:T]

            dve.wait_ge(S("zeroed"), 6)
            r = result(("es", 0), 0, L)
            d.sig(TT(sm, r, rL, ALU.mult), "small_ready")
            feed(("es", 0))

            def convolve(tile, ct, dst):
                r = result(tile, 0, L)
                s_ = scr2[:, CONVS.index(tile) % 2, :]
                d.settle()
                d.sig(TT(s_[:, 3:3 + L], r, rL, ALU.mult), "out_taken")
                feed(tile)
                d.settle()
                d.step(TS(dst, s_[:, 0:L], pcol("even_conv", ct), pcol("even_conv_b", ct), ALU.mult, ALU.add))
                for j in (1, 2, 3):
                    d.settle()
                    ins = STT(out=dst, in0=s_[:, j:L + j], scalar=pcol("even_conv", 10 * j + ct), in1=dst,
                              op0=ALU.mult, op1=ALU.add)
                    d.sig(ins, "xconv") if j == 3 else d.step(ins)

            def z_full(tile, dst, src=None, name="dve_step", rows=slice(0, P)):
                src = dst if src is None else src
                n = HALF[tile]
                dve.wait_ge(S("z_tanh"), n + 1)
                d.sig(STT(out=dst, in0=th[rows, n % 2, :], scalar=1.0, in1=src, op0=ALU.add, op1=ALU.mult), name)

            def decay_sum(i):
                dve.wait_ge(S("gate_ln"), i + 1)
                d.settle()
                d.step(TS(small2, bank(4 + i % 2)[:, 0:L], pcol("gate_b", i), 0.0, ALU.add, ALU.min))
                d.settle()
                d.step(TT(small2, small2, gtmp[:, i % 2, :], ALU.subtract))
                d.settle()
                d.sig(V.tensor_tensor_scan(gcs[:, i, :], mask("restart"), small2, 0.0, ALU.mult, ALU.add), "decay_sum")

            d.settle()
            d.step(TS(small2[0:16, :], sm[0:16, :], pcol("dt_bias")[0:16], 0.0, ALU.add, ALU.max))
            dve.wait_ge(S("dt_ln"), 1)
            d.settle()
            d.step(TT(scans[0:16, :], small2[0:16, :], small1[0:16, :], ALU.add))
            d.step(TS(acol[0:16, 1:2], acol[0:16, 0:1], -1.0, None, ALU.mult))
            d.settle()
            d.step(TS(small2[0:16, :], scans[0:16, :], acol[0:16, 1:2], None, ALU.mult))
            d.settle()
            d.sig(V.tensor_tensor_scan(acs[0:16, :], mask("ones")[0:16, 0:L], small2[0:16, :], 0.0, ALU.mult, ALU.add),
                  "acs_ready")
            d.settle()
            d.sig(V.tensor_copy(scans[LR_ROW:LR_ROW + 16, :], acs[0:16, :]), "scans_ready")
            halves = prm[:, PARAMS["even_conv"]:PARAMS["even_conv"] + 50]
            d.step(TS(halves, halves, 0.5, None, ALU.mult))
            convolve(("eb", 0), 8, bT)
            decay_sum(0)
            decay_sum(1)
            convolve(("ec", 0), 9, cvo)
            decay_sum(2)
            decay_sum(3)
            z_full(("eb", 0), bT, name="xsilu")
            convolve(("ex", 0), 0, xs[:, 0, :])
            for g_ in range(2):
                r = slice(64 * g_, 64 * g_ + 64)
                z_full(("ec", 0), cT[r, g_, :], cvo[r], "xsilu" if g_ else "dve_step", r)
            convolve(("ex", 1), 1, xs[:, 1, :])
            z_full(("ex", 0), xs[:, 0, :], name="xsilu")
            z_full(("ex", 1), xs[:, 1, :], name="xsilu")
            dve.wait_ge(S("rinv_T"), 2)
            d.settle()
            d.step(V.tensor_copy(rcol[:, 0:1], bank(6)[:, 0:1]))
            d.step(V.tensor_copy(rcol[:, 1:2], bank(6)[:, P:P + 1]))
            d.sig(V.tensor_copy(tkc, bank(6)[:, 256:512].rearrange("p (a b) -> p a b", a=2)), "tkc_ready")
            for g_ in range(2):
                dve.wait_ge(S("cb_ready"), g_ + 1)
                d.sig(TT(cb[:, g_, :], bank(4 + g_)[:, 0:CC], mask("causal"), ALU.mult), "cb_taken")

            def z_half(tile, dst):
                r = result(tile, 0, L)
                d.settle()
                d.sig(STT(out=dst, in0=r, scalar=0.5, in1=rL, op0=ALU.mult, op1=ALU.mult), "z_half")
                feed(tile)

            def ssd_args(u):
                dve.wait_ge(S("xT_ready"), u + 1)
                d.settle()
                dtv = tkc[:, :, 2 * u:2 * u + 2].unsqueeze(3).to_broadcast([P, 2, 2, 64])
                d.sig(TT(xd.rearrange("p t (h c) -> p t h c", c=64),
                         bank(5)[:, 0:L].rearrange("p (t h c) -> p t h c", t=2, c=64), dtv, ALU.mult), "xd_ready")
                dve.wait_ge(S(f"spread{u % 2}"), 16 * (u // 2 + 1))
                for h in (2 * u, 2 * u + 1):
                    for t in range(2):
                        w_ = slice(0, L) if t == 0 else slice(L, CC)
                        ins = TS(dec[:, h % 2, w_], bc[:, u % 2, h % 2, P * t:L],
                                 tkc[:, t, LR_ROW + h:LR_ROW + h + 1], 0.0, ALU.subtract, ALU.min)
                        d.sig(ins, "decay_arg") if t else d.step(ins)

            def ssd_y(u):
                dve.wait_ge(S("y_ready"), u + 1)
                d.sig(STT(out=xs[:, u, :], in0=xs[:, u, :], scalar=pcol("d_skip", u), in1=bank(5)[:, 0:L],
                          op0=ALU.mult, op1=ALU.add), "ssd_y")

            def gate_y(u):
                d.settle()
                d.sig(TT(xs[:, u, :], xs[:, u, :], zs[:, u % 2, :], ALU.mult), "yz_ready")

            def ssd_low(u):
                dve.wait_ge(S("ye_hi"), u + 1)
                d.sig(STT(out=elo[:, u, :], in0=xs[:, u, :], scalar=pcol("ssd_norm", u),
                          in1=ehi[:, u, :].bitcast(F32), op0=ALU.mult, op1=ALU.subtract), "ye_split")

            def gla_args(p):
                need(dve, "sc_ready", p - 1)
                k = p % 2
                gv = gcs[:, p, :].rearrange("p (c t) -> p c t", t=64)
                d.step(TT(ka[:, k, :].rearrange("p (c t) -> p c t", t=64), gv,
                          gv[:, :, 32:33].to_broadcast([P, 4, 64]), ALU.subtract))
                d.sig(TT(kb[:, k, :].rearrange("p (c t) -> p c t", t=64), gv[:, :, 63:64].to_broadcast([P, 4, 64]),
                         gv, ALU.subtract), "gla_arg")

            def gla_scores(p):
                dve.wait_ge(S("sc_ready"), p + 1)
                for t in range(2):
                    ins = V.copy_predicated(sc[:, t, :], mask("chunk").bitcast(I32), bank(6)[:, L * t:L * t + L])
                    d.sig(ins, "sc_taken") if t else d.step(ins)

            def gla_states(p):
                dve.wait_ge(S("kv_ready"), p + 1)
                kv = [bank((6, 4)[n % 2])[:, P * n:P * n + P] for n in range(3)]
                d.step(V.tensor_copy(st[:, 0, :], kv[0]))
                for n in (1, 2):
                    d.settle()
                    ins = STT(out=st[:, n, :], in0=st[:, n - 1, :], scalar=eg[:, p % 2, 64 * n + 63:64 * n + 64],
                              in1=kv[n], op0=ALU.mult, op1=ALU.add)
                    d.sig(ins, "st_ready") if n == 2 else d.step(ins)

            def gla_norm(p):
                dve.wait_ge(S("gla_rms"), p + 1)
                for hh in range(2):
                    w_ = slice(L * hh, L * hh + L)
                    ins = STT(out=orv[:, w_], in0=bank(6)[:, w_], scalar=pcol("gla_norm"), in1=orv[:, w_],
                              op0=ALU.mult, op1=ALU.mult)
                    d.sig(ins, "gla_on") if hh else d.step(ins)
                d.settle()
                for hh in range(2):
                    g_ = gs[:, (2 * p + hh) % 4, :]
                    d.sig(TT(g_, g_, orv[:, L * hh:L * hh + L], ALU.mult), "gla_og")

            def gla_low(p):
                for h in (2 * p, 2 * p + 1):
                    dve.wait_ge(S("go_hi"), h + 1)
                    d.sig(TT(elo[:, KT + h, :], gs[:, h % 4, :], ehi[:, KT + h, :].bitcast(F32), ALU.subtract),
                          "go_split")

            for p in range(4):
                u, k = 2 * p, p % 2
                r = result(("eq", p), 0, L)
                need(dve, "gla_qk", p - 1)
                d.sig(STT(out=e_q[:, k, :], in0=r, scalar=0.125, in1=rL, op0=ALU.mult, op1=ALU.mult), "out_taken")
                if p:
                    gla_states(p - 1)
                feed(("eq", p))
                if p:
                    z_full(("ex", u + 1), xs[:, u + 1, :], name="xsilu")
                ssd_args(u)
                r = result(("ek", p), 0, L)
                d.sig(TT(e_k[:, k, :], r, rL, ALU.mult), "out_taken")
                feed(("ek", p))
                if p == 0:
                    dve.wait_ge(S("zeroed"), 9)
                gla_args(p)
                need(dve, "gla_o", p - 1)
                for o in range(2):
                    r = result(("ev", p), o, L)
                    d.sig(TS(vb[:, k, o, :], r, rcol[:, o:o + 1], None, ALU.mult), "out_taken")
                feed(("ev", p))
                ssd_y(u)
                z_half(("ez", u), zs[:, 0, :])
                if p:
                    gla_norm(p - 1)
                ssd_args(u + 1)
                z_half(("eg", u), gs[:, u % 4, :])
                z_full(("ez", u), zs[:, 0, :])
                gate_y(u)
                z_full(("eg", u), gs[:, u % 4, :])
                dve.wait_ge(S("klT_ready"), p + 1)
                d.sig(V.tensor_copy(klt[:, k].rearrange("p a b -> p (a b)"), bank(6)[:, 0:L]), "klt_ready")
                if p:
                    gla_low(p - 1)
                if p < 3:
                    convolve(("ex", u + 2), u + 2, xs[:, u + 2, :])
                z_half(("ez", u + 1), zs[:, 1, :])
                ssd_low(u)
                if p < 3:
                    z_full(("ex", u + 2), xs[:, u + 2, :], name="xsilu")
                z_half(("eg", u + 1), gs[:, (u + 1) % 4, :])
                ssd_y(u + 1)
                z_full(("ez", u + 1), zs[:, 1, :])
                gate_y(u + 1)
                z_full(("eg", u + 1), gs[:, (u + 1) % 4, :])
                ssd_low(u + 1)
                gla_scores(p)
                if p < 3:
                    convolve(("ex", u + 3), u + 3, xs[:, u + 3, :])
            gla_states(3)

            def residual(stage):
                for i in range(KT):
                    r = result((stage, i), 0, L)
                    d.settle()
                    d.sig(TT(H[:, i, META:T], r, H[:, i, META:T], ALU.add), "h_ready")
                    feed((stage, i))

            dve.wait_ge(S("rms_ready"), 6)
            for i in range(KT):
                r = result(("eo1", i), 0, L)
                t_ = zs[:, i % 2, :]
                d.settle()
                d.sig(TT(t_, r, rpost[:, 0:L], ALU.mult), "eo1_taken")
                feed(("eo1", i))
                if i == 0:
                    gla_norm(3)
                if i == 1:
                    gla_low(3)
                d.settle()
                d.step(TT(H[:, i, META:T], H[:, i, META:T], t_, ALU.add))
            residual("eo2")
            x_low("odd_norm", META, 3 * KT)
            dve.wait_ge(S("rms_ready"), 7)
            d.settle()
            for i in range(KT):
                r = result(("mk", i), 0, L)
                d.sig(TT(mkT[:, i, :], r, rL, ALU.mult), "out_taken")
                feed(("mk", i))
            dve.wait_ge(S("rinv_T"), 3)
            d.step(V.tensor_copy(rcol[:, 0:1], bank(6)[:, 0:1]))
            d.sig(V.tensor_copy(rcol[:, 1:2], bank(6)[:, P:P + 1]), "rcol3")
            d.settle()
            for i in range(4):
                for o in range(2):
                    r = result(("mv", i), o, L)
                    d.sig(TS(mval[:, o, 256 * i:256 * i + 256], r, rcol[:, o:o + 1], None, ALU.mult), "out_taken")
                feed(("mv", i))
            dve.wait_ge(S("zeroed"), 10)

            def scores_max(h):
                s_, t_ = pr[:, h % 4, :], mst[:, h % 4, :]
                dve.wait_ge(S("s_ready"), h + 1)
                d.settle()
                d.sig(TT(s_, bank(4)[:, 0:CC], mask("causal_neg"), ALU.add), "s_taken")
                d.settle()
                d.step(V.tensor_reduce(t_[:, 4:5], s_[:, 0:P], AX_X, ALU.max))
                d.step(V.tensor_reduce(t_[:, 5:6], s_[:, P:CC], AX_X, ALU.max))
                d.settle()
                d.sig(TS(t_[:, 0:2], t_[:, 4:6], -1.0, None, ALU.mult), "m_max")

            def normalise(h):
                s_, t_ = pr[:, h % 4, :], mst[:, h % 4, :]
                dve.wait_ge(S("m_exp"), h + 1)
                d.settle()
                d.step(V.reciprocal(t_[:, 6:8], t_[:, 2:4]))
                d.settle()
                for t in range(2):
                    w_ = slice(0, P) if t == 0 else slice(P, CC)
                    ins = TS(s_[:, w_], s_[:, w_], t_[:, 6 + t:7 + t], None, ALU.mult)
                    d.sig(ins, "p_ready") if t else d.step(ins)

            def m_low(j):
                dve.wait_ge(S("mo_hi"), j + 1)
                d.sig(TT(elo[:, j, :], mo[:, j % 2, :], ehi[:, j, :].bitcast(F32), ALU.subtract), "mo_split")

            for i in range(KT + 3):
                if 2 <= i <= KT + 1:
                    normalise(2 * i - 4)
                if i < KT:
                    r = result(("mq", i), 0, L)
                    d.settle()
                    for e in range(2):
                        rows = slice(64 * e, 64 * e + 64)
                        ins = STT(out=mqp[rows, i % 2, e, :], in0=r[rows], scalar=0.125, in1=rL[rows],
                                  op0=ALU.mult, op1=ALU.mult)
                        d.sig(ins, "out_taken") if e else d.step(ins)
                    feed(("mq", i))
                if 2 <= i <= KT + 1:
                    normalise(2 * i - 3)
                if i >= 4:
                    m_low(i - 4)
                if 1 <= i <= KT:
                    scores_max(2 * i - 2)
                if i >= 3:
                    j = i - 3
                    dve.wait_ge(S("m_av"), 2 * j + 2)
                    d.settle()
                    d.sig(TT(mo[:, j % 2, :], bank(7)[:, 0:L], mzs[:, j % 4, :], ALU.mult), "mo_ready")
                j = i - MZ_LAG
                if 0 <= j < KT:
                    r = result(("mz", j), 0, L)
                    d.settle()
                    d.sig(STT(out=mz[:, j % 2, :], in0=r, scalar=0.5, in1=rL, op0=ALU.mult, op1=ALU.mult), "mz_half")
                    feed(("mz", j))
                if 1 <= i <= KT:
                    scores_max(2 * i - 1)
                if 0 <= j < KT:
                    dve.wait_ge(S("mz_tanh"), j + 1)
                    d.step(STT(out=mzs[:, j % 4, :], in0=mzs[:, j % 4, :], scalar=1.0, in1=mz[:, j % 2, :],
                               op0=ALU.add, op1=ALU.mult))
            m_low(KT - 1)
            residual("mo")
            dve.wait_ge(S("rms_ready"), 8)
            d.settle()
            for i in range(KT):
                d.sig(STT(out=mout[:, i, 0:L], in0=H[:, i, META:T], scalar=pcol("final_norm", i), in1=rL,
                          op0=ALU.mult, op1=ALU.mult), "final")

        @block.tensor
        def _(pe):
            n_sig = {}
            mm, tr = nc.tensor.matmul, nc.tensor.transpose
            ident = mask("identity")
            ones = mask("ones")[:, 0:P]

            def bank_free(n):
                if n >= 4:
                    pe.wait_ge(S(taken[n - 4][0]), taken[n - 4][1])

            def project(tile, hi, lo, a, b, ready=None, toks=None):
                f, nb, no = FIRST_BLOCK[tile], BLOCKS_OF[tile], FIRST_OUT[tile]
                for o in range(OUTS_OF[tile]):
                    bank_free(no + o)
                step = 1 if toks is None else 2
                for j in range(0, nb, step):
                    c, kt = (f + j) // BPC, j // step
                    at = (c % RING) * CW + ((f + j) % BPC) * P
                    if (f + j) % BPC == 0 or j == 0:
                        pe.wait_ge(S("lo_ready"), c + 1)
                    if ready is not None:
                        ready(kt)
                    first, last = j == 0, j + step >= nb
                    outs = [None] if toks is None else toks
                    for o, tok in enumerate(outs):
                        for n, (w_, x_) in enumerate(((whi, hi), (whi, lo), (wlo, hi))):
                            wt = w_[:, at:at + step * P]
                            s0, s1 = first and n == 0, last and n == 2
                            if tok is None:
                                ins = mm(bank(no % 4)[:, 0:b - a], wt, x_[:, kt, a:b], start=s0, stop=s1)
                            else:
                                t0, t1 = tok
                                ins = mm(bank((no + o) % 4)[0:t1 - t0, 0:2 * P], x_[:, kt, t0:t1], wt,
                                         start=s0, stop=s1)
                        if last:
                            ins.then_inc(S("out_ready"), 1)
                    if (f + j + step) % BPC == 0 and not last:
                        ins.then_inc(S("chunk_read"), 1)

            def sums(base, a, b, nth):
                for kt in range(KT):
                    pe.wait_ge(S("sq_ready"), base + kt + 1)
                    ins = mm(bank(SSB)[:, 0:b - a], ones, sq[:, kt, a:b], start=kt == 0, stop=kt == KT - 1)
                ins.then_inc(S("sums_ready"), 1)

            def x_ready(base):
                return lambda kt: pe.wait_ge(S("x_split"), base + kt + 1)

            def rinv_by_token(starts, nth):
                pe.wait_ge(S("rms_ready"), nth)
                for n, (t0, t1) in enumerate(starts):
                    ins = tr(bank(6)[0:t1 - t0, P * n:P * n + P], rinv[:, t0:t1], ident)
                return ins

            toks3 = [(0, P), (P, 2 * P), (2 * P, T)]
            toksL = [(META, META + P), (META + P, T)]
            project(("k", 0), xhi, xlo, 0, T, x_ready(0))
            pe.wait_ge(S("load_masks"), 16)
            sums(0, 0, T, 1)
            for i in range(1, KT):
                project(("k", i), xhi, xlo, 0, T)
            rinv_by_token(toks3, 1).then_inc(S("rinv_T"), 1)
            for i in range(4):
                project(("v", i), xhi, xlo, 0, T, toks=toks3)

            def scores(h):
                p, e = h // 2, h % 2
                if e == 0:
                    pe.wait_ge(S("out_taken"), Q_TAKEN[p])
                need(pe, "loga_taken", h - 1)
                for n, (c0, k0, t0) in enumerate(SEG):
                    ins = mm(bank(4 + e)[:, c0:c0 + T - t0], keysT[:, p, k0:k0 + P], qpair[:, p % 2, e, t0:T],
                             start=n == 0, stop=n == 2, skip_group_check=True)
                ins.then_inc(S("z_ready"), 1)

            def survive(h):
                pe.wait_ge(S("f_ready"), h + 1)
                zb, f_ = bank(4 + h % 2), fz[:, h % 2, :]
                later = mask("neg_ones")
                mm(zb[:, 0:ZC], mask("neg_tri"), f_, start=False, stop=False, skip_group_check=True)
                c1, c2 = SEG[1][0], SEG[2][0]
                mm(zb[:, 128 - TA:NA], later, f_[:, c1:c2], start=False, stop=False, skip_group_check=True)
                mm(zb[:, 256 - TA:NA], later, f_[:, c2:ZC], start=False, stop=False, skip_group_check=True)
                mm(zb[:, c1 + 128:c2], later, f_[:, c2:ZC], start=False, stop=True,
                   skip_group_check=True).then_inc(S("loga_ready"), 1)

            def attend(h):
                p, e = h // 2, h % 2
                pe.wait_ge(S("a_ready"), h + 1)
                need(pe, "att_split", p - 1)
                rows = slice(64 * e, 64 * e + 64)
                for n, (c0, k0, t0) in enumerate(SEG):
                    ins = mm(bank(6 + p % 2)[rows, t0 - TA:NA], vals[:, n, 64 * h:64 * h + 64],
                             aw[:, h % 2, c0:c0 + T - t0], start=n == 0, stop=n == 2, skip_group_check=True)
                ins.then_inc(S("av_ready"), 1)

            Q_TAKEN = [taken[FIRST_OUT["q", p]][1] for p in range(KT)]
            pe.wait_ge(S("zeroed"), 3)
            for p in range(KT):
                project(("q", p), xhi, xlo, TA, T)
                if p >= 2:
                    attend(2 * p - 4)
                    survive(2 * p - 3)
                if p:
                    scores(2 * p - 2)
                project(("c", p), xhi, xlo, TC, T)
                project(("h", p), xhi, xlo, TC, T)
                if p >= 2:
                    attend(2 * p - 3)
                if p:
                    survive(2 * p - 2)
                    scores(2 * p - 1)
                project(("b", p), xhi, xlo, TA, T)
            attend(12)
            survive(13)
            scores(14)
            project(("gc", 0), xhi, xlo, TA, T)
            attend(13)
            survive(14)
            scores(15)
            project(("ga", 0), xhi, xlo, TA, T)

            def conv_projection(i):
                project(("pc", i), yhi[:, CONV], ylo[:, CONV], 0, NA,
                        (lambda kt: pe.wait_ge(S("conv_split"), kt + 1)) if i == 0 else None)

            conv_projection(0)
            attend(14)
            survive(15)
            project(("gc", 1), xhi, xlo, TA, T)
            attend(15)
            project(("ga", 1), xhi, xlo, TA, T)
            conv_projection(1)
            for i in range(0, KT, 2):
                for j in (i, i + 1) if i else ():
                    project(("gc", j), xhi, xlo, TA, T)
                    project(("ga", j), xhi, xlo, TA, T)
                    conv_projection(j)
                for j in (i, i + 1):
                    project(("pa", j), yhi[:, ATT], ylo[:, ATT], 0, NA,
                            (lambda kt: pe.wait_ge(S("att_split"), kt + 1)) if j == 0 else None)

            def out_sums(base, i, t0):
                pe.wait_ge(S("sq_ready"), base + i + 1)
                ins = mm(bank(SSB)[:, 0:T - t0], ones, sq[:, i, t0:T], start=i == 0, stop=i == KT - 1)
                if i == KT - 1:
                    ins.then_inc(S("sums_ready"), 1)

            for i in range(KT):
                project(("wo", i), yhi[:, MERGED], ylo[:, MERGED], 0, NA,
                        (lambda kt: pe.wait_ge(S("merged_split"), kt + 1)) if i == 0 else None)
                if i:
                    out_sums(KT, i - 1, TA)
            out_sums(KT, KT - 1, TA)
            project(("fu", 0), xhi, xlo, TA, T, x_ready(KT))
            sums(2 * KT, TA, T, 3)
            for i in range(FT):
                if i:
                    project(("fu", i), xhi, xlo, TA, T)
                project(("fg", i), xhi, xlo, META, T)
            for i in range(KT):
                project(("fd", i), fhi, flo, 0, L,
                        (lambda kt: pe.wait_ge(S("ffn_split"), kt + 1)) if i == 0 else None)
                if i:
                    out_sums(3 * KT, i - 1, META)
            out_sums(3 * KT, KT - 1, META)

            project(("es", 0), xhi, xlo, META, T, x_ready(2 * KT))
            sums(4 * KT, META, T, 5)

            def low_rank(i):
                need(pe, "decay_sum", i - 1)
                mm(bank(4 + i % 2)[:, 0:L], gw2[:, P * i:P * i + P], sm, start=True, stop=True).then_inc(S("lowrank"), 1)

            project(("eb", 0), xhi, xlo, META, T)
            pe.wait_ge(S("load_gate"), 16)
            pe.wait_ge(S("small_ready"), 1)
            low_rank(0)
            low_rank(1)
            project(("ec", 0), xhi, xlo, META, T)
            project(("ex", 0), xhi, xlo, META, T)
            low_rank(2)
            low_rank(3)
            project(("ex", 1), xhi, xlo, META, T)
            project(("eq", 0), xhi, xlo, META, T)
            rinv_by_token(toksL, 5)
            pe.wait_ge(S("scans_ready"), 1)
            for t in range(2):
                ins = tr(bank(6)[:, 256 + P * t:256 + P * t + P], scans[:, P * t:P * t + P], ident)
            ins.then_inc(S("rinv_T"), 1)
            project(("ek", 0), xhi, xlo, META, T)
            pe.wait_ge(S("xsilu"), 2)
            pe.wait_ge(S("decay_sum"), 4)
            for g_ in range(2):
                for t in range(2):
                    ins = mm(bank(4 + g_)[:, (0, L)[t]:(L, CC)[t]], bT[:, P * t:P * t + P], cT[:, g_, P * t:L],
                             start=t == 0, stop=t == 1, skip_group_check=True)
                ins.then_inc(S("cb_ready"), 1)

            def turn_x(u):
                pe.wait_ge(S("xsilu"), 2 + u + 1)
                need(pe, "ssd_y", u)
                for t in range(2):
                    ins = tr(bank(5)[:, P * t:P * t + P], xs[:, u, P * t:P * t + P], ident)
                ins.then_inc(S("xT_ready"), 1)

            def ssd_heads(u):
                pe.wait_ge(S("xd_ready"), u + 1)
                for h in (2 * u, 2 * u + 1):
                    pe.wait_ge(S("m_ready"), h + 1)
                    rows = slice(64 * (h % 2), 64 * (h % 2) + 64)
                    for t in range(2):
                        ins = mm(bank(5)[rows, P * t:L], xd[:, t, rows], dec[:, h % 2, (0, L)[t]:(L, CC)[t]],
                                 start=t == 0, stop=t == 1, skip_group_check=True)
                ins.then_inc(S("y_ready"), 1)

            def ssd_squares(u):
                pe.wait_ge(S("sqy_ready"), u + 1)
                mm(bank(SSB)[:, 0:L], ones, sqy[:, u % 2, :], start=u == 0, stop=u == KT - 1).then_inc(
                    S("sum_part") if u < KT - 1 else S("sums_ready"), 1)

            def turn_keys(p):
                pe.wait_ge(S("gla_kl"), p + 1)
                need(pe, "gla_on", p)
                for t in range(2):
                    ins = tr(bank(6)[:, P * t:P * t + P], kb[:, p % 2, P * t:P * t + P], ident)
                ins.then_inc(S("klT_ready"), 1)

            def gla_scores(p):
                pe.wait_ge(S("gla_qk"), p + 1)
                pe.wait_ge(S("klt_ready"), p + 1)
                for t in range(2):
                    ins = mm(bank(6)[:, L * t:L * t + L], ka[:, p % 2, P * t:P * t + P],
                             qe[:, p % 2, :, P * t:P * t + P], start=True, stop=True)
                ins.then_inc(S("sc_ready"), 1)

            def gla_kv(p):
                pe.wait_ge(S("sc_taken"), p + 1)
                need(pe, "gla_rms", p)
                for n in range(3):
                    rows = slice(64 * (n % 2), 64 * (n % 2) + 64)
                    for e in range(2):
                        ins = mm(bank((6, 4)[n % 2])[64 * e:64 * e + 64, P * n:P * n + P],
                                 klt[rows, p % 2, n // 2, 64 * e:64 * e + 64], vb[rows, p % 2, n // 2, P * e:P * e + P],
                                 start=True, stop=True, skip_group_check=True)
                ins.then_inc(S("kv_ready"), 1)

            def gla_out(p):
                pe.wait_ge(S("st_ready"), p + 1)
                ob = bank(6).rearrange("p (e t) -> p e t", e=2)
                for t in range(2):
                    for e in range(2):
                        mm(ob[:, e, P * t:P * t + P], vb[:, p % 2, t, P * e:P * e + P], sc[:, t, P * e:P * e + P],
                           start=t == 0 and e == 0, stop=False, skip_group_check=True)
                for n in (1, 2, 3):
                    ins = mm(ob[:, :, 64 * n:64 * n + 64], st[:, n - 1, :], qg[:, p % 2, :, 64 * n:64 * n + 64],
                             start=False, stop=n == 3, skip_group_check=True)
                ins.then_inc(S("gla_o"), 1)

            def gla_sums(p):
                pe.wait_ge(S("gla_sq"), p + 1)
                mm(bank(4), ones, osq, start=True, stop=True).then_inc(S("gla_sums"), 1)

            pe.wait_ge(S("cb_taken"), 2)
            pe.wait_ge(S("tkc_ready"), 1)
            for p in range(4):
                u = 2 * p
                if p:
                    project(("eq", p), xhi, xlo, META, T)
                turn_x(u)
                if p:
                    ssd_squares(u - 1)
                    gla_kv(p - 1)
                if p:
                    project(("ek", p), xhi, xlo, META, T)
                    gla_out(p - 1)
                project(("ev", p), xhi, xlo, META, T, toks=toksL)
                ssd_heads(u)
                if p:
                    gla_sums(p - 1)
                project(("ez", u), xhi, xlo, META, T)
                turn_x(u + 1)
                project(("eg", u), xhi, xlo, META, T)
                turn_keys(p)
                if p < 3:
                    project(("ex", u + 2), xhi, xlo, META, T)
                project(("ez", u + 1), xhi, xlo, META, T)
                ssd_heads(u + 1)
                ssd_squares(u)
                project(("eg", u + 1), xhi, xlo, META, T)
                gla_scores(p)
                if p < 3:
                    project(("ex", u + 3), xhi, xlo, META, T)
            gla_kv(3)

            def ssd_out(i):
                project(("eo1", i), ehi, elo, 0, L,
                        (lambda kt: pe.wait_ge(S("ye_split"), kt + 1)) if i == 0 else None)

            ssd_out(0)
            ssd_squares(KT - 1)
            gla_out(3)
            ssd_out(1)
            gla_sums(3)
            for i in range(2, KT):
                ssd_out(i)
            for i in range(KT):
                project(("eo2", i), ehi[:, KT:], elo[:, KT:], 0, L,
                        (lambda kt: pe.wait_ge(S("go_split"), kt + 1)) if i == 0 else None)
            project(("mk", 0), xhi, xlo, META, T, x_ready(3 * KT))
            sums(5 * KT, META, T, 7)
            for i in range(1, KT):
                project(("mk", i), xhi, xlo, META, T)
            rinv_by_token(toksL, 7).then_inc(S("rinv_T"), 1)
            for i in range(4):
                project(("mv", i), xhi, xlo, META, T, toks=toksL)
            pe.wait_ge(S("rcol3"), 1)
            MQ = [taken[FIRST_OUT["mq", p]][1] for p in range(KT)]

            def m_scores(h):
                i, e = h // 2, h % 2
                if e == 0:
                    pe.wait_ge(S("out_taken"), MQ[i])
                need(pe, "s_taken", h)
                for t in range(2):
                    ins = mm(bank(4)[:, (0, P)[t]:(P, CC)[t]], mqp[:, i % 2, e, P * t:P * t + P],
                             mkT[:, i, 0:P * (t + 1)], start=t == 0, stop=t == 1, skip_group_check=True)
                ins.then_inc(S("s_ready"), 1)

            def m_turn(h):
                pe.wait_ge(S("p_ready"), h + 1)
                need(pe, "p_taken", h - 1)
                for n in range(3):
                    ins = tr(bank(5 + h % 2)[:, P * n:P * n + P], pr[:, h % 4, P * n:P * n + P], ident)
                ins.then_inc(S("p_T"), 1)

            def m_attend(h):
                i, e = h // 2, h % 2
                pe.wait_ge(S("p_taken"), h + 1)
                need(pe, "mo_ready", i)
                rows = slice(64 * e, 64 * e + 64)
                b_ = bank(7)
                mm(b_[rows, 0:L], mval[:, 0, 64 * h:64 * h + 64], prT[:, e, 0:L], start=True, stop=False,
                   skip_group_check=True)
                mm(b_[rows, P:L], mval[:, 1, 64 * h:64 * h + 64], prT[:, e, L:CC], start=False, stop=True,
                   skip_group_check=True).then_inc(S("m_av"), 1)

            pe.wait_ge(S("zeroed"), 10)
            for i in range(KT + 3):
                if i < KT:
                    project(("mq", i), xhi, xlo, META, T)
                if i >= 3:
                    m_attend(2 * (i - 3) + 1)
                if 1 <= i <= KT:
                    m_scores(2 * i - 2)
                if 2 <= i <= KT + 1:
                    m_turn(2 * i - 4)
                if MZ_LAG <= i < KT + MZ_LAG:
                    project(("mz", i - MZ_LAG), xhi, xlo, META, T)
                if 1 <= i <= KT:
                    m_scores(2 * i - 1)
                if 2 <= i <= KT + 1:
                    m_attend(2 * i - 4)
                if 2 <= i <= KT + 1:
                    m_turn(2 * i - 3)
            for i in range(KT):
                project(("mo", i), ehi, elo, 0, L,
                        (lambda kt: pe.wait_ge(S("mo_split"), kt + 1)) if i == 0 else None)
                if i:
                    out_sums(6 * KT, i - 1, META)
            out_sums(6 * KT, KT - 1, META)


MASKS = {}
MASK_COLS = 0
for _name, _n in (("identity", P), ("ones", L), ("neg_ones", P), ("neg_tri", P), ("stick", ZC), ("stick_neg", ZC),
                  ("causal", CC), ("causal_neg", CC), ("restart", L), ("chunk", L), ("eps", 1), ("one", 1)):
    MASKS[_name] = (MASK_COLS, _n)
    MASK_COLS += _n
ARENA = 17600


def mask_array():
    m = np.zeros((P, MASK_COLS), np.float32)

    def put(name, a):
        o, n = MASKS[name]
        m[:, o:o + n] = a

    r = np.arange(P)[:, None]
    put("identity", np.eye(P))
    put("ones", 1.0)
    put("neg_ones", -1.0)
    put("neg_tri", -(r >= np.arange(P)[None]).astype(np.float32))
    ok = np.concatenate([(k0 + r) < (t0 + np.arange(T - t0))[None] for c0, k0, t0 in SEG], 1)
    put("stick", ok)
    put("stick_neg", np.where(ok, 0.0, -30000.0))
    put("causal", np.concatenate([r <= np.arange(L)[None], r <= np.arange(P)[None]], 1))
    qk = np.concatenate([np.arange(P)[None] <= r, np.arange(L)[None] <= r + P], 1)
    put("causal_neg", np.where(qk, 0.0, -1e30))
    put("restart", (np.arange(L) % 64 != 0)[None])
    j, i = np.arange(P)[:, None], np.arange(P)[None]
    blk = ((j // 64 == i // 64) & (j <= i)).astype(np.float32)
    put("chunk", np.concatenate([blk, blk], 1))
    put("eps", EPS)
    put("one", 1.0)
    return m


def kernel(**inputs):
    import concourse.bacc as bacc
    from concourse.bass_utils import run_bass_kernel_spmd

    f = {k: np.asarray(v) for k, v in inputs.items()}
    mats = {k: f[k][0] for k in ("w_in", "w_proj_conv", "w_proj_attn", "w_out", "w_up_gate", "w_down", "even_w_in_2",
                                 "even_w_out_2", "odd_w_in_2", "odd_w_out_2")}
    small = np.zeros((D, P), np.float32)
    small[:, 0:16] = mats["even_w_in_2"][:, E_DT:E_DT + 16]
    small[:, LR_ROW:LR_ROW + 16] = mats["even_w_in_2"][:, E_LR:E_LR + 16]
    mats["small"] = small
    weights = np.empty((NCHUNKS, P, CW), np.float32)
    b = 0
    for _, _, blocks, _ in STREAM:
        for name, kt, col in blocks:
            weights[b // BPC, :, (b % BPC) * P:(b % BPC) * P + P] = mats[name][kt * P:kt * P + P, col:col + P]
            b += 1
    tokens = np.concatenate([f["meta_tokens"], f["x"][0]], 0)
    xT = np.ascontiguousarray(tokens.T.reshape(KT, P, T).transpose(1, 0, 2)).reshape(P, KT * T)
    prm = np.zeros((P, NPARAM), np.float32)

    def put(name, a):
        a = np.asarray(a).reshape(-1)
        n = a.size // P
        prm[:, PARAMS[name]:PARAMS[name] + n] = a.reshape(n, P).T

    for name, key in (("g_pre_mix",) * 2, ("g_post_mix",) * 2, ("g_pre_ffn",) * 2, ("g_post_ffn",) * 2,
                      ("even_norm", "even_norm_2"), ("ssd_norm", "even_ssd_norm_2"), ("odd_norm", "odd_norm_2"),
                      ("final_norm", "final_norm_2"), ("conv_mix", "conv_w_mix"), ("b_gate", "b_gate"),
                      ("conv_ffn", "conv_w_ffn"), ("even_conv", "even_conv_w_2"), ("even_conv_b", "even_conv_b_2"),
                      ("gate_b", "even_gate_b_2"), ("gla_norm", "even_gla_norm_2")):
        put(name, f[key])
    put("d_skip", np.repeat(f["even_d_skip_2"][0], 64))
    prm[0:16, PARAMS["dt_bias"]] = f["even_dt_bias_2"][0]
    prm[0:16, PARAMS["a_log"]] = f["even_a_log_2"][0]
    gw = np.zeros((P, 512), np.float32)
    gw[LR_ROW:LR_ROW + 16] = f["even_gate_w2_2"][0]

    nc = bacc.Bacc("TRN2", target_bir_lowering=False, num_devices=1)
    arrays = {"xT_in": xT, "params_in": prm, "weights_in": weights, "masks_in": mask_array(), "gate_w2_in": gw}
    aps = {k: nc.dram_tensor(k, a.shape, F32, kind="ExternalInput").ap() for k, a in arrays.items()}
    out = nc.dram_tensor("out", (P, KT, L), F32, kind="ExternalOutput").ap()
    scratch = nc.dram_tensor("decay_rows", (HEADS, L), F32).ap()
    build(nc, aps["xT_in"], aps["params_in"], aps["weights_in"], aps["masks_in"], aps["gate_w2_in"], out, scratch)
    r = run_bass_kernel_spmd(nc, [arrays], core_ids=[0])
    got = r.results[0]["out"]
    return np.ascontiguousarray(got.transpose(2, 1, 0)).reshape(1, L, D)
```
